# Optimizing a Trainium2 kernel written in Bass

```python
import numpy as np
import jax, jax.numpy as jnp
from jax import lax

D_MODEL = 1024
BATCH = 1
SEQ = 512
DEPTH = 1
DEC_BATCH = 8
DEC_SEQ = 8
PAST_LEN = 1024
PAGE_SIZE = 128

C_CONV = 512
CONV_K = 31
N_HEADS = 8
N_KV = 2
HEAD_DIM = 64
HPG = N_HEADS // N_KV
CMP_BLOCK = 32
CMP_STRIDE = 16
CMP_RATIO = CMP_BLOCK // CMP_STRIDE
SEL_BLOCK = 64
N_SEL = 16
WINDOW = 512
Q_BLOCK = 128
ROPE_THETA = 10000.0
FORCE_BONUS = 1000.0
NEG_INF = -1e30
N_GROUPS = 4
EXP_PER_GROUP = 8
N_EXPERTS = N_GROUPS * EXP_PER_GROUP
TOP_K_IN_GROUP = 2
D_EXPERT = 128
EPS = 1e-6
KV_W = N_KV * HEAD_DIM
IN_SPLITS = (2 * C_CONV, N_HEADS * HEAD_DIM, KV_W, KV_W, KV_W, KV_W, KV_W, KV_W, 3 * N_HEADS, 2 * D_MODEL)
IN_COLS = sum(IN_SPLITS)

kernel_name = 'hybrid_conformer_nsa_hmoe_step'

def rms_norm(x, g):
    xf = x.astype(jnp.float32)
    y = xf * lax.rsqrt(jnp.mean(xf * xf, axis=-1, keepdims=True) + EPS)
    return (y * g.astype(jnp.float32)).astype(x.dtype)

def rope(x, pos):
    half = HEAD_DIM // 2
    inv_freq = ROPE_THETA ** (-jnp.arange(half, dtype=jnp.float32) * 2.0 / HEAD_DIM)
    ang = pos.astype(jnp.float32)[:, None] * inv_freq[None, :]
    cos = jnp.cos(ang)[None, :, None, :]
    sin = jnp.sin(ang)[None, :, None, :]
    xf = x.astype(jnp.float32)
    x1, x2 = xf[..., :half], xf[..., half:]
    return jnp.concatenate([x1 * cos - x2 * sin, x2 * cos + x1 * sin], axis=-1).astype(x.dtype)

def project_in(xn, w_in):
    B, T, _ = xn.shape
    cuts = [int(c) for c in np.cumsum(IN_SPLITS)[:-1]]
    u, q, kc, vc, ks, vs, kw, vw, ng, mg = jnp.split(xn @ w_in, cuts, axis=-1)
    heads = lambda a, n: a.reshape(B, T, n, HEAD_DIM)
    return (u, heads(q, N_HEADS), heads(kc, N_KV), heads(vc, N_KV), heads(ks, N_KV), heads(vs, N_KV),
            heads(kw, N_KV), heads(vw, N_KV),
            jax.nn.sigmoid(ng.reshape(B, T, N_HEADS, 3)),
            jax.nn.sigmoid(mg.reshape(B, T, 2, D_MODEL)))

def conv_module(u, buf, w_dw, b_dw, n_g, n_b, w_out):
    a = u[..., :C_CONV] * jax.nn.sigmoid(u[..., C_CONV:])
    full = jnp.concatenate([buf, a], axis=1)
    c = lax.conv_general_dilated(full, w_dw[:, None, :], (1,), 'VALID',
                                 dimension_numbers=('NWC', 'WIO', 'NWC'),
                                 feature_group_count=C_CONV) + b_dw
    cf = c.astype(jnp.float32)
    mu = jnp.mean(cf, axis=-1, keepdims=True)
    var = jnp.mean(jnp.square(cf - mu), axis=-1, keepdims=True)
    cn = (cf - mu) * lax.rsqrt(var + EPS) * n_g.astype(jnp.float32) + n_b.astype(jnp.float32)
    y = jax.nn.silu(cn).astype(u.dtype) @ w_out
    return y, full[:, -(CONV_K - 1):]

def compress(k_raw, w1, b1, w2):
    B, T, G, Dh = k_raw.shape
    nb = (T - CMP_BLOCK) // CMP_STRIDE + 1
    n_str = nb + CMP_RATIO - 1
    s = k_raw[:, :n_str * CMP_STRIDE].reshape(B, n_str, CMP_STRIDE, G, Dh)
    w1r = w1.reshape(CMP_RATIO, CMP_STRIDE, Dh, Dh)
    pre = jnp.einsum('bnlgd,lde->bnge', s[:, 0:nb], w1r[0]) + b1
    for r in range(1, CMP_RATIO):
        pre = pre + jnp.einsum('bnlgd,lde->bnge', s[:, r:r + nb], w1r[r])
    return jnp.einsum('bnge,ef->bngf', jax.nn.silu(pre), w2)

def block_overlap(nc, ns):
    i = np.arange(nc)[:, None]
    j = np.arange(ns)[None, :]
    ov = (i * CMP_STRIDE < (j + 1) * SEL_BLOCK) & (i * CMP_STRIDE + CMP_BLOCK > j * SEL_BLOCK)
    return jnp.asarray(ov.astype(np.float32))

def nsa_attend(q, q_rot, pos, kc, vc, gather_sel, ns, kw, vw, pos_w, gates):
    B, Q = q.shape[0], q.shape[1]
    scale = HEAD_DIM ** -0.5
    qg = q.reshape(B, Q, N_KV, HPG, HEAD_DIM)
    qrg = q_rot.reshape(B, Q, N_KV, HPG, HEAD_DIM)
    t = pos
    nc = kc.shape[1]
    c_end = jnp.arange(nc) * CMP_STRIDE + CMP_BLOCK - 1
    c_ok = c_end[None, :] <= t[:, None]
    s_c = jnp.einsum('bqghd,bngd->bqghn', qg, kc).astype(jnp.float32) * scale
    s_c = jnp.where(c_ok[None, :, None, None, :], s_c, NEG_INF)
    p_c = jax.nn.softmax(s_c, axis=-1) * jnp.any(c_ok, axis=-1)[None, :, None, None, None]
    o_c = jnp.einsum('bqghn,bngd->bqghd', p_c.astype(vc.dtype), vc)
    imp = jnp.einsum('bqghn,nj->bqgj', p_c, block_overlap(nc, ns))
    j = jnp.arange(ns)
    cur = t // SEL_BLOCK
    forced = (j[None, :] == 0) | (j[None, :] == cur[:, None]) | (j[None, :] == cur[:, None] - 1)
    blk_ok = j[None, :] * SEL_BLOCK <= t[:, None]
    imp = jnp.where(blk_ok[None, :, None, :], imp + FORCE_BONUS * forced[None, :, None, :], NEG_INF)
    _, idx = lax.top_k(imp, min(N_SEL, ns))
    ks, vs = gather_sel(idx)
    tok = idx[..., None] * SEL_BLOCK + jnp.arange(SEL_BLOCK)
    tok_ok = tok <= t[None, :, None, None, None]
    s_s = jnp.einsum('bqghd,bqgkld->bqghkl', qrg, ks).astype(jnp.float32) * scale
    s_s = jnp.where(tok_ok[:, :, :, None], s_s, NEG_INF)
    p_s = jax.nn.softmax(s_s.reshape(B, Q, N_KV, HPG, -1), axis=-1).reshape(s_s.shape)
    o_s = jnp.einsum('bqghkl,bqgkld->bqghd', p_s.astype(vs.dtype), vs)
    w_ok = (pos_w[None, :] <= t[:, None]) & (t[:, None] - pos_w[None, :] < WINDOW) & (pos_w[None, :] >= 0)
    s_w = jnp.einsum('bqghd,bwgd->bqghw', qrg, kw).astype(jnp.float32) * scale
    s_w = jnp.where(w_ok[None, :, None, None, :], s_w, NEG_INF)
    p_w = jax.nn.softmax(s_w, axis=-1)
    o_w = jnp.einsum('bqghw,bwgd->bqghd', p_w.astype(vw.dtype), vw)
    g = gates.reshape(B, Q, N_KV, HPG, 3)
    o = g[..., 0:1] * o_c + g[..., 1:2] * o_s + g[..., 2:3] * o_w
    return o.reshape(B, Q, N_HEADS, HEAD_DIM)

def merge_out(y_conv, y_nsa, mg, w_o):
    return (mg[:, :, 0] * y_conv + mg[:, :, 1] * y_nsa) @ w_o

def mixer_prompt(xn, w_in, conv_w, cmp_w, w_nsa_out, w_o):
    B, T, _ = xn.shape
    pos = jnp.arange(T)
    u, q, kc_r, vc_r, ks_r, vs, kw_r, vw, ng, mg = project_in(xn, w_in)
    y_conv, conv_state = conv_module(u, jnp.zeros((B, CONV_K - 1, C_CONV), u.dtype), *conv_w)
    q_rot, ks, kw = rope(q, pos), rope(ks_r, pos), rope(kw_r, pos)
    kc = compress(kc_r, *cmp_w[:3])
    vc = compress(vc_r, *cmp_w[3:])
    ns = T // SEL_BLOCK
    kb = ks.reshape(B, ns, SEL_BLOCK, N_KV, HEAD_DIM)
    vb = vs.reshape(B, ns, SEL_BLOCK, N_KV, HEAD_DIM)
    b_ix = jnp.arange(B)[:, None, None, None]
    g_ix = jnp.arange(N_KV)[None, None, :, None]

    def gather_sel(idx):
        return kb[b_ix, idx, :, g_ix, :], vb[b_ix, idx, :, g_ix, :]

    pad = ((0, 0), (WINDOW, 0), (0, 0), (0, 0))
    kw_pad, vw_pad = jnp.pad(kw, pad), jnp.pad(vw, pad)

    def block(i):
        start = i * Q_BLOCK
        sl = lambda a: lax.dynamic_slice_in_dim(a, start, Q_BLOCK, axis=1)
        kwb = lax.dynamic_slice_in_dim(kw_pad, start, Q_BLOCK + WINDOW, axis=1)
        vwb = lax.dynamic_slice_in_dim(vw_pad, start, Q_BLOCK + WINDOW, axis=1)
        pos_b = start + jnp.arange(Q_BLOCK)
        pos_w = start - WINDOW + jnp.arange(Q_BLOCK + WINDOW)
        return nsa_attend(sl(q), sl(q_rot), pos_b, kc, vc, gather_sel, ns, kwb, vwb, pos_w, sl(ng))

    o = lax.map(block, jnp.arange(T // Q_BLOCK))
    o = jnp.moveaxis(o, 0, 1).reshape(B, T, N_HEADS * HEAD_DIM)
    out = merge_out(y_conv, o @ w_nsa_out, mg, w_o)
    wb = min(WINDOW, T)
    return out, (kc_r, vc_r, ks, vs, kw[:, T - wb:], vw[:, T - wb:], conv_state)

def mixer_sample(xn, ck_cmp, cv_cmp, ck_sel, cv_sel, sk_win, sv_win, s_conv, page_table,
                 w_in, conv_w, cmp_w, w_nsa_out, w_o):
    B, T, _ = xn.shape
    past = page_table.shape[1] * PAGE_SIZE
    pos = past + jnp.arange(T)
    u, q, kc_r, vc_r, ks_r, vs, kw_r, vw, ng, mg = project_in(xn, w_in)
    y_conv, conv_state = conv_module(u, s_conv, *conv_w)
    q_rot, ks, kw = rope(q, pos), rope(ks_r, pos), rope(kw_r, pos)

    def paged(pool):
        return pool[page_table].reshape(B, past, N_KV, HEAD_DIM)

    kc = compress(jnp.concatenate([paged(ck_cmp), kc_r], axis=1), *cmp_w[:3])
    vc = compress(jnp.concatenate([paged(cv_cmp), vc_r], axis=1), *cmp_w[3:])
    ns_past = past // SEL_BLOCK
    n_new = -(-T // SEL_BLOCK)
    bpp = PAGE_SIZE // SEL_BLOCK
    pool_blocks = lambda p: p.reshape(p.shape[0], bpp, SEL_BLOCK, N_KV, HEAD_DIM)
    pad_new = ((0, 0), (0, n_new * SEL_BLOCK - T), (0, 0), (0, 0))
    new_blocks = lambda a: jnp.pad(a, pad_new).reshape(B, n_new, SEL_BLOCK, N_KV, HEAD_DIM)
    kp, vp = pool_blocks(ck_sel), pool_blocks(cv_sel)
    kn, vn = new_blocks(ks), new_blocks(vs)
    b_ix = jnp.arange(B)[:, None, None, None]
    g_ix = jnp.arange(N_KV)[None, None, :, None]

    def gather_sel(idx):
        in_past = (idx < ns_past)[..., None, None]
        jp = jnp.minimum(idx, ns_past - 1)
        jn = jnp.clip(idx - ns_past, 0, n_new - 1)
        page = page_table[b_ix, jp // bpp]
        sub = jp % bpp
        k_g = jnp.where(in_past, kp[page, sub, :, g_ix, :], kn[b_ix, jn, :, g_ix, :])
        v_g = jnp.where(in_past, vp[page, sub, :, g_ix, :], vn[b_ix, jn, :, g_ix, :])
        return k_g, v_g

    wb = sk_win.shape[1]
    kw_all = jnp.concatenate([sk_win, kw], axis=1)
    vw_all = jnp.concatenate([sv_win, vw], axis=1)
    pos_w = past - wb + jnp.arange(wb + T)
    o = nsa_attend(q, q_rot, pos, kc, vc, gather_sel, ns_past + n_new, kw_all, vw_all, pos_w, ng)
    out = merge_out(y_conv, o.reshape(B, T, N_HEADS * HEAD_DIM) @ w_nsa_out, mg, w_o)
    return out, (kc_r, vc_r, ks, vs, kw_all[:, T:], vw_all[:, T:], conv_state)

def hier_moe(xn, w_rg, b_rg, w_re, b_re, w_gate, w_up, w_down):
    shp = xn.shape
    xf = xn.reshape(-1, D_MODEL)
    lg = (xf @ w_rg).astype(jnp.float32) + b_rg.astype(jnp.float32)
    p_grp = jax.nn.softmax(lg, axis=-1)
    g_star = jnp.argmax(lg, axis=-1)
    le = ((xf @ w_re).astype(jnp.float32) + b_re.astype(jnp.float32)).reshape(-1, N_GROUPS, EXP_PER_GROUP)
    le_g = jnp.take_along_axis(le, g_star[:, None, None], axis=1)[:, 0]
    top_v, top_i = lax.top_k(le_g, TOP_K_IN_GROUP)
    w_tok = jax.nn.softmax(top_v, axis=-1) * jnp.take_along_axis(p_grp, g_star[:, None], axis=1)
    eid = g_star[:, None] * EXP_PER_GROUP + top_i
    comb = jnp.sum(jax.nn.one_hot(eid, N_EXPERTS, dtype=jnp.float32) * w_tok[..., None], axis=1)
    hid = jax.nn.silu(jnp.einsum('nd,edf->nef', xf, w_gate)) * jnp.einsum('nd,edf->nef', xf, w_up)
    y = jnp.einsum('nef,efd->nd', hid * comb[..., None].astype(hid.dtype), w_down)
    return y.reshape(shp)

def setup_inputs(seed: int = 0) -> dict:
    key = jax.random.key(seed)
    keys = jax.random.split(key, 40)
    n_pages = PAST_LEN // PAGE_SIZE
    n_phys = (DEC_BATCH * n_pages * 5) // 4
    wb = min(WINDOW, PAST_LEN)
    L = DEPTH

    def nrm(i, shape, scale):
        return jax.random.normal(keys[i], shape, jnp.float32) * scale

    pool = (L, n_phys, PAGE_SIZE, N_KV, HEAD_DIM)
    page_table = jax.random.permutation(keys[9], n_phys)[:DEC_BATCH * n_pages].reshape(DEC_BATCH, n_pages).astype(jnp.int32)
    return {
        'x_prompt': nrm(0, (BATCH, SEQ, D_MODEL), 1.0),
        'x_sample': nrm(1, (DEC_BATCH, DEC_SEQ, D_MODEL), 1.0),
        'cache_k_cmp': nrm(2, pool, 1.0),
        'cache_v_cmp': nrm(3, pool, 1.0),
        'cache_k_sel': nrm(4, pool, 1.0),
        'cache_v_sel': nrm(5, pool, 1.0),
        'state_k_win': nrm(6, (L, DEC_BATCH, wb, N_KV, HEAD_DIM), 1.0),
        'state_v_win': nrm(7, (L, DEC_BATCH, wb, N_KV, HEAD_DIM), 1.0),
        'state_conv': nrm(8, (L, DEC_BATCH, CONV_K - 1, C_CONV), 0.5),
        'page_table': page_table,
        'g_mix': 1.0 + nrm(10, (L, D_MODEL), 0.01),
        'w_in': nrm(11, (L, D_MODEL, IN_COLS), D_MODEL ** -0.5),
        'w_dw': nrm(12, (L, CONV_K, C_CONV), CONV_K ** -0.5),
        'b_dw': nrm(13, (L, C_CONV), 0.01),
        'conv_norm_g': 1.0 + nrm(14, (L, C_CONV), 0.01),
        'conv_norm_b': nrm(15, (L, C_CONV), 0.01),
        'w_conv_out': nrm(16, (L, C_CONV, D_MODEL), C_CONV ** -0.5),
        'w_ck1': nrm(17, (L, CMP_BLOCK, HEAD_DIM, HEAD_DIM), (CMP_BLOCK * HEAD_DIM) ** -0.5),
        'b_ck1': nrm(18, (L, HEAD_DIM), 0.01),
        'w_ck2': nrm(19, (L, HEAD_DIM, HEAD_DIM), HEAD_DIM ** -0.5),
        'w_cv1': nrm(20, (L, CMP_BLOCK, HEAD_DIM, HEAD_DIM), (CMP_BLOCK * HEAD_DIM) ** -0.5),
        'b_cv1': nrm(21, (L, HEAD_DIM), 0.01),
        'w_cv2': nrm(22, (L, HEAD_DIM, HEAD_DIM), HEAD_DIM ** -0.5),
        'w_nsa_out': nrm(23, (L, N_HEADS * HEAD_DIM, D_MODEL), (N_HEADS * HEAD_DIM) ** -0.5),
        'w_o': nrm(24, (L, D_MODEL, D_MODEL), D_MODEL ** -0.5),
        'g_ffn': 1.0 + nrm(25, (L, D_MODEL), 0.01),
        'w_rg': nrm(26, (L, D_MODEL, N_GROUPS), D_MODEL ** -0.5),
        'b_rg': nrm(27, (L, N_GROUPS), 0.01),
        'w_re': nrm(28, (L, D_MODEL, N_EXPERTS), D_MODEL ** -0.5),
        'b_re': nrm(29, (L, N_EXPERTS), 0.01),
        'w_gate': nrm(30, (L, N_EXPERTS, D_MODEL, D_EXPERT), D_MODEL ** -0.5),
        'w_up': nrm(31, (L, N_EXPERTS, D_MODEL, D_EXPERT), D_MODEL ** -0.5),
        'w_down': nrm(32, (L, N_EXPERTS, D_EXPERT, D_MODEL), D_EXPERT ** -0.5),
        'g_final': 1.0 + nrm(33, (D_MODEL,), 0.01),
    }

def reference(x_prompt, x_sample, cache_k_cmp, cache_v_cmp, cache_k_sel, cache_v_sel, state_k_win, state_v_win,
              state_conv, page_table, g_mix, w_in, w_dw, b_dw, conv_norm_g, conv_norm_b, w_conv_out,
              w_ck1, b_ck1, w_ck2, w_cv1, b_cv1, w_cv2, w_nsa_out, w_o, g_ffn, w_rg, b_rg, w_re, b_re,
              w_gate, w_up, w_down, g_final):
    h_p, h_s = x_prompt, x_sample
    per_layer = []
    for l in range(DEPTH):
        conv_w = (w_dw[l], b_dw[l], conv_norm_g[l], conv_norm_b[l], w_conv_out[l])
        cmp_w = (w_ck1[l], b_ck1[l], w_ck2[l], w_cv1[l], b_cv1[l], w_cv2[l])
        moe_w = (w_rg[l], b_rg[l], w_re[l], b_re[l], w_gate[l], w_up[l], w_down[l])
        mix_p, st_p = mixer_prompt(rms_norm(h_p, g_mix[l]), w_in[l], conv_w, cmp_w, w_nsa_out[l], w_o[l])
        h_p = h_p + mix_p
        h_p = h_p + hier_moe(rms_norm(h_p, g_ffn[l]), *moe_w)
        mix_s, st_s = mixer_sample(rms_norm(h_s, g_mix[l]), cache_k_cmp[l], cache_v_cmp[l], cache_k_sel[l],
                                   cache_v_sel[l], state_k_win[l], state_v_win[l], state_conv[l], page_table,
                                   w_in[l], conv_w, cmp_w, w_nsa_out[l], w_o[l])
        h_s = h_s + mix_s
        h_s = h_s + hier_moe(rms_norm(h_s, g_ffn[l]), *moe_w)
        per_layer.append(st_p + st_s)
    (k_cmp_p, v_cmp_p, k_sel_p, v_sel_p, k_win_p, v_win_p, conv_p,
     k_cmp_s, v_cmp_s, k_sel_s, v_sel_s, k_win_s, v_win_s, conv_s) = [jnp.stack(s) for s in zip(*per_layer)]
    y_prompt = rms_norm(h_p, g_final)
    y_sample = rms_norm(h_s, g_final)
    return (y_prompt, y_sample, k_cmp_p, v_cmp_p, k_sel_p, v_sel_p, k_win_p, v_win_p, conv_p,
            k_cmp_s, v_cmp_s, k_sel_s, v_sel_s, k_win_s, v_win_s, conv_s)


_drawn_inputs = setup_inputs


def setup_inputs(seed=0):
    import zlib

    import numpy as np

    out = dict(_drawn_inputs(seed))
    spreads = {}
    factors = {'g_mix': 4.276,
     'conv_norm_g': 22.788,
     'b_ck1': 32.357,
     'b_cv1': 64.0,
     'b_rg': 17.725,
     'g_final': 31.926,
     'b_dw': 8.0,
     'conv_norm_b': 8.0,
     'g_ffn': 4.747,
     'b_re': 8.0}
    for name, (base, spread) in spreads.items():
        noise = np.random.default_rng([zlib.crc32(name.encode()), seed]).standard_normal(out[name].shape)
        drawn = base * np.exp(spread * noise) if base else spread * noise
        out[name] = __import__('jax').numpy.asarray(drawn.astype(out[name].dtype))
    for name, factor in factors.items():
        out[name] = (out[name] * factor).astype(out[name].dtype)
    return out
```

```python
from contextlib import ExitStack

import numpy as np

import concourse.bass as bass
from concourse import mybir

F32 = mybir.dt.float32
BF16 = mybir.dt.bfloat16
I32 = mybir.dt.int32
U16 = mybir.dt.uint16
ALU = mybir.AluOpType
ACT = mybir.ActivationFunctionType
AX = mybir.AxisListType

P = 128
D = 1024
KD = D // P
SEQ, DB, DS = 512, 8, 8
NS_TOK = DB * DS
T = SEQ + NS_TOK
NT = (T + P - 1) // P
TS = [min(P, T - P * i) for i in range(NT)]
QT = SEQ // P
C = 512
CC = C // P
TAPS = 31
PAD = TAPS - 1
HD = 64
NKV = 2
HPG = 4
NH = NKV * HPG
PAST = 1024
PAGE = 128
NPG = PAST // PAGE
NPHYS = DB * NPG * 5 // 4
WIN = 512
WB = WIN // P
SELB = 64
NSELB = PAST // SELB + 1
NCP = (SEQ - 32) // 16 + 1
NCS = (PAST + DS - 32) // 16 + 1
STR_S = DB * PAST // 16
STR_P = SEQ // 16
STR = STR_S + STR_P
NE = 32
NG = 4
EPG = 8
NR = NG + NE
F = 128
EPS = 1e-6
NEG = -1e30
U0, Q0, KV0, NG0, MG0, NCOL = 0, 1024, 1536, 2304, 2328, 4376
KVN = MG0 - KV0

SLOTS = 4
J_NORM = 0
J_KV = J_NORM + KD
J_GLU = J_KV + NT
J_KT = J_GLU + 2 * CC
J_CST = J_KT + 2
J_WDW = J_CST + 1
J_CSO = J_WDW + 1
J_MG = J_CSO + 1
J_CMP = J_MG + 2 * KD
J_CMPV = J_CMP + DB + 4
J_Q = J_CMPV + DB + 5
Q_PER = 32
J_S = J_Q + HPG * Q_PER
S_PER = 12
J_LN = J_S + (DB // 2) * S_PER
J_OUT = J_LN + 2
J_WO = J_OUT + 2 * KD
J_N2 = J_WO + NT
J_RT = J_N2 + KD
J_POS = J_RT + 1
J_MOE = J_POS + 1
E_PER = 8
BR = 64
N_OVER = (2 * T - 1) // BR + 1
NBLK = NE + N_OVER
NPAIR = NBLK // 2
NUSUAL = NE // 2 + 3
MAX_OVER = 2 * T // BR


def build(nc, a):
    o = a["outs"]
    with ExitStack() as ctx:
        def sem(name):
            return ctx.enter_context(nc.semaphore(name))

        def sb(name, shape, dt=F32):
            return ctx.enter_context(nc.sbuf_tensor(name, shape, dt))

        ps = ctx.enter_context(nc.psum_tensor("ps", [P, SLOTS, 1024], F32))

        def slot(j):
            return ps[:, j % SLOTS, :]

        filled = [sem(f"filled{s}") for s in range(SLOTS)]
        emptied = [sem(f"emptied{s}") for s in range(SLOTS)]

        def count(j, it, per):
            return j // SLOTS if it is None else it * (per // SLOTS) + j // SLOTS

        def highest(eng, sems, wants):
            for s in range(SLOTS):
                mine = [c for slot_, c in wants if slot_ == s]
                if mine:
                    last = max(range(len(mine)), key=lambda n: mine[n][0])
                    eng.wait_ge(sems[s], mine[last][1])

        def want(j, it, per, more):
            return j % SLOTS, (j // SLOTS + more, count(j, it, per) + more)

        def claim(pe, j, it=None, per=0, after=()):
            wants = [want(x, it, per, 1) for x in after]
            if j >= SLOTS:
                wants.append(want(j, it, per, 0))
            highest(pe, emptied, wants)

        def take(eng, *jobs, it=None, per=0):
            highest(eng, filled, [want(j, it, per, 1) for j in jobs])

        def result_of(eng, *jobs, it=None, per=0):
            highest(eng, emptied, [want(j, it, per, 1) for j in jobs])

        def fill(ins, j):
            ins.then_inc(filled[j % SLOTS], 1)

        def give(ins, j):
            ins.then_inc(emptied[j % SLOTS], 1)

        class Steps:

            def __init__(self, eng, s):
                self.eng, self.s, self.n, self.base = eng, s, 0, None

            def do(self, ins):
                self.n += 1
                ins.then_inc(self.s, 1)
                self.sync()

            def mark(self, ins):
                self.n += 1
                ins.then_inc(self.s, 1)

            def sync(self):
                v = self.n if self.base is None else self.base + self.n
                self.eng.wait_ge(self.s, v)

            def begin(self, it, per):
                self.per, self.n0 = per, self.n
                self.base = it * per

            def end(self, trips):
                assert self.n - self.n0 == self.per, (self.s, self.n - self.n0)
                self.n = self.n0 + self.per * trips
                self.base = None

        h = sb("h", [P, NT, D])
        xT = sb("xT", [P, KD, T])
        mgT = sb("mgT", [P, 2 * KD, T])
        keep1 = sb("keep1", [P, NT * KVN + NT * 2 * P])
        keep2 = sb("keep2", [P, CC * (PAD + SEQ) + CC * DB * (PAD + DS) + 2 * T])
        cv = sb("cv", [P, CC, T])
        oT = sb("oT", [P, HPG, T])
        kcT = sb("kcT", [P, STR])
        vcS = sb("vcS", [HD, DB, P])
        vcP = sb("vcP", [32, P])
        qs = sb("qs", [P, 2, HPG, NS_TOK])
        gates = sb("gates", [P, NT, 3 * NH])
        gS = sb("gS", [P, DB // 2, 3])
        ident = sb("ident", [P, P])
        identb = sb("identb", [P, P], BF16)
        causal = sb("causal", [P, P], BF16)
        cmask = sb("cmask", [P, QT, 32], BF16)
        rmask = sb("rmask", [P, 2, DS], BF16)
        perm = sb("perm", [P, P])
        hsum = sb("hsum", [P, P])
        ovl = sb("ovl", [HD, NSELB])
        jidx = sb("jidx", [P, NSELB])
        bonus = sb("bonus", [P, NSELB])
        anyok = sb("anyok", [P, 1])
        onesC = sb("onesC", [P, P])
        cosT = sb("cosT", [P, T])
        sinT = sb("sinT", [P, T])
        cosR = sb("cosR", [P, NT, 32])
        sinR = sb("sinR", [P, NT, 32])
        gmix = sb("gmix", [P, KD])
        gffn = sb("gffn", [P, KD])
        gffn2 = sb("gffn2", [P, KD])
        wdw = sb("wdw", [P, CC, TAPS])
        bdw = sb("bdw", [P, CC])
        cng = sb("cng", [P, CC])
        cnb = sb("cnb", [P, CC])
        b1 = sb("b1", [HD, 2])
        w2 = sb("w2", [HD, 2, HD])
        pidx = sb("pidx", [P, DB // 2 + 2 * DB], I32)
        gidx = sb("gidx", [P, DB // 2 + 2 * DB], I32)
        pmod = sb("pmod", [P, 4])
        ss = sb("ss", [P, 3, 8])
        rs = sb("rs", [P, 3, 8])
        mhalf = sb("mhalf", [P, 8])
        dest = sb("dest", [P, NT, 2], I32)
        eid = sb("eid", [P, 2 * N_OVER], I32)
        ARENA = 13900
        arena = sb("arena", [P, ARENA])

        def cut(at, *shape, parts=P, base=None):
            base = arena[:, :] if base is None else base
            n = 1
            for x in shape:
                n *= x
            v = base[0:parts, at:at + n]
            if len(shape) == 2:
                v = v.rearrange("p (a b) -> p a b", b=shape[1])
            if len(shape) == 3:
                v = v.rearrange("p (a b c) -> p a b c", b=shape[1], c=shape[2])
            if len(shape) == 4:
                v = v.rearrange("p (a b c d) -> p a b c d", b=shape[1], c=shape[2], d=shape[3])
            return v

        k1, k2 = keep1[:, :], keep2[:, :]
        mg_flat = mgT[:, :, :].rearrange("p a b -> p (a b)")
        oT_flat = oT[:, :, :].rearrange("p a b -> p (a b)")
        xT_flat = xT[:, :, :].rearrange("p a b -> p (a b)")
        kv = cut(0, NT, KVN, base=k1)
        rot = cut(NT * KVN, NT, 2, P, base=k1)
        aP = cut(0, CC, PAD + SEQ, base=k2)
        aS = cut(CC * (PAD + SEQ), CC, DB, PAD + DS, base=k2)
        kT = cut(CC * (PAD + SEQ) + CC * DB * (PAD + DS), 2, T, base=k2)

        xs = cut(0, NT, D)
        wkv = cut(0, KD, KVN, base=mg_flat)
        wring = [cut(5120 + 1024 * s, KD, P) for s in range(4)]
        sg = [cut(9216 + T * s, T) for s in range(2)]
        rtmp = cut(9216 + 2 * T, 2, 2, NKV, 32)
        cso = cut(9216 + 2 * T + 256, 2, C)
        anew = cut(11648, CC, NS_TOK)
        wdr = cut(1024, C, parts=TAPS)
        cst = cut(0, 2, C)
        XT = cut(0, NKV, KD, STR)
        raw = [cut(8704 + 2048 * s, 16, P) for s in range(2)]
        w1 = cut(8704 + 4096, KD, P)
        upper = cut(0, NKV, STR, parts=HD, base=oT_flat)
        pre = cut(2 * STR, NKV, STR, parts=HD, base=oT_flat)
        wq = [cut(11776 + 1024 * s, KD, P) for s in range(2)]
        qT = cut(0, T)
        qrot = cut(576, T)
        qtmp = cut(1152, 2, T)
        Pb = [cut(2304 + 1024 * s, 2, 512) for s in range(4)]
        PT = [cut(6400 + 1024 * s, 2, 512) for s in range(2)]
        Pc = [cut(8448 + 64 * s, 2, 32) for s in range(2)]
        PcT = cut(8576, 2, P, parts=32)
        otok = cut(8832, QT, P)
        smx = cut(9344, 12, 2)
        sms = cut(9376, QT, NKV, 3)
        coef = cut(9408, NKV, 3)
        kraw = [cut(9440 + 1024 * s, NPG, P) for s in range(2)]
        ksT = [cut(1024 * s, NPG * P) for s in range(2)]
        vsel = [cut(2048 + 1024 * s, NPG, P) for s in range(2)]
        kwraw = cut(4096, 2, WB, P)
        kwT = cut(5120, 2, WIN)
        vwin = cut(6144, 2, WB, P)
        PTs = cut(7168, 12, P)
        PTn = cut(8704, 3, P, parts=HD)
        qbd = cut(11500, 2, 2, NKV * HPG * DS)
        vst = cut(11760, 2, 3, P, parts=HD)
        kdyn = cut(9100, 2, 80)
        PW = PAST + WIN + 2 * DS + NCS
        CMP0 = PW - NCS
        Ps = cut(0, PW, base=xT_flat)
        snew = cut(PW, 2 * DS, base=xT_flat)
        sv = cut(PW + 16, 64, base=xT_flat)
        imp = cut(PW + 80, 6, NSELB, base=xT_flat)
        pcn = cut(PW + 200, P, base=xT_flat)
        wco = cut(0, CC, D, base=k1)
        wno = [cut(1024 * c, D, base=k2) for c in range(3)] + [cut(12700, D)]
        gfin = cut(3072, D, base=k2)
        sq = cut(8192, CC, T)
        rstd = cut(8192 + CC * T, T)
        mt = cut(11072, 2, T)
        wo = cut(0, KD, D)
        xs2 = cut(0, NT, D, base=k1)
        wr = cut(0, KD, NR, base=mg_flat)
        lg = cut(288, NT, NR, base=mg_flat)
        brow = cut(632, NR, base=mg_flat)
        N_CIDX = NG + EPG + NE + N_OVER + MAX_OVER
        cidx = cut(670, N_CIDX, base=mg_flat)
        rt = cut(780, 26, NT * NE, base=mg_flat)
        place = cut(8050, 2 * NT * NE, base=mg_flat)
        grid = cut(5140, NE * max(N_OVER, MAX_OVER), base=mg_flat)
        run = [cut(5760 + 48 * s, 16 + NE, base=mg_flat) for s in range(2)]
        xeT = [cut(5860 + 1024 * s, KD, P, base=mg_flat) for s in range(2)]
        tri = cut(7910, P, base=mg_flat)
        cv_flat = cv[:, :, :].rearrange("p a b -> p (a b)")
        ye = [cut(1024 * s, D, base=cv_flat) for s in range(2)]
        sil = [cut(2048 + P * s, P, base=cv_flat) for s in range(2)]
        xe = [cut(1024 * s, D, base=k2) for s in range(3)] + [cut(0, D, base=oT_flat)]
        hid = [cut(1024 + P * s, P, base=oT_flat) for s in range(2)]
        got = [cut(0, NT, D, base=k1), cut(0, NT, D)]
        wgate = [cut(6144 * s, 2, KD, P) for s in range(2)]
        wup = [cut(6144 * s + 2048, 2, KD, P) for s in range(2)]
        wdn = [cut(6144 * s + 4096, 2, D) for s in range(2)]
        s_first = sem("s_first")
        s_const = sem("s_const")
        s_x = sem("s_x")
        s_wkv = sem("s_wkv")
        s_wring = [sem(f"s_wring{s}") for s in range(4)]
        s_sq = sem("s_sq")
        s_pow = sem("s_pow")
        s_xs = sem("s_xs")
        s_dve = sem("s_dve")
        s_act = sem("s_act")
        s_pool = sem("s_pool")
        s_gates = sem("s_gates")
        s_idx = sem("s_idx")
        s_rope = sem("s_rope")
        s_pads = sem("s_pads")
        s_kvout = sem("s_kvout")
        s_cst = sem("s_cst")
        s_cso = sem("s_cso")
        s_moved = sem("s_moved")
        s_conv = sem("s_conv")
        s_gs = sem("s_gs")
        s_w1 = sem("s_w1")
        s_anew = sem("s_anew")
        s_raw = [sem(f"s_raw{s}") for s in range(2)]
        s_upper = sem("s_upper")
        s_silu = sem("s_silu")
        s_wq = [sem(f"s_wq{s}") for s in range(2)]
        s_qrot = sem("s_qrot")
        s_max = sem("s_max")
        s_kin = [sem(f"s_kin{s}") for s in range(2)]
        s_vin = [sem(f"s_vin{s}") for s in range(2)]
        s_kw = sem("s_kw")
        s_vw = sem("s_vw")
        s_qbd = sem("s_qbd")
        s_expc = sem("s_expc")
        s_pcn = sem("s_pcn")
        s_snew = sem("s_snew")
        s_maxs = sem("s_maxs")
        s_exps = sem("s_exps")
        s_scaled = sem("s_scaled")
        s_wout = sem("s_wout")
        s_wo = sem("s_wo")
        s_xc = sem("s_xc")
        s_sqd = sem("s_sqd")
        s_cn = sem("s_cn")
        s_silc = sem("s_silc")
        s_var = sem("s_var")
        s_merged = sem("s_merged")
        s_wr = sem("s_wr")
        s_sub = sem("s_sub")
        s_ex = sem("s_ex")
        s_we = [sem(f"s_we{s}") for s in range(2)]
        s_wd = [sem(f"s_wd{s}") for s in range(2)]
        s_sil = sem("s_sil")
        s_hid = sem("s_hid")
        s_zero = sem("s_zero")
        s_dest = sem("s_dest")
        s_eid = sem("s_eid")
        s_scat = sem("s_scat")
        s_xe = [sem(f"s_xe{s}") for s in range(4)]
        s_ye = [sem(f"s_ye{s}") for s in range(2)]
        s_got = [sem(f"s_got{i}") for i in range(NT)]
        s_final = sem("s_final")
        s_gfin = sem("s_gfin")
        s_out = sem("s_out")
        s_gsw = sem("s_gsw")

        s_kcout = sem("s_kcout")
        s_vst = sem("s_vst")
        s_anyok = sem("s_anyok")
        s_hy = sem("s_hy")
        N_KVOUT = 4 + 4 + 2 * DB

        block = ctx.enter_context(nc.Block())
        w_in_v = a["w_in"][0].rearrange("(k p) n -> p k n", p=P)
        strides_of = {n: a[n].rearrange("l n (s r) g d -> (l n s) (r g d)", r=16) for n in ("cache_k_cmp", "cache_v_cmp")}
        quads_of = {n: a[n].rearrange("l n (s r) g d -> (l n s) (r g d)", r=4) for n in ("cache_k_sel", "cache_v_sel")}
        rows = lambda t: t[0].rearrange("b r g d -> (b r) (g d)")

        consts = [
            (gffn[:, :], a["g_ffn"].rearrange("l (k p) -> p (l k)", p=P)),
            (gffn2[:, :], a["g_ffn"].rearrange("l (p k) -> (l p) k", p=P)),
            (bdw[:, :], a["b_dw"].rearrange("l (c p) -> p (l c)", p=P)),
            (cng[:, :], a["conv_norm_g"].rearrange("l (c p) -> p (l c)", p=P)),
            (cnb[:, :], a["conv_norm_b"].rearrange("l (c p) -> p (l c)", p=P)),
            (b1[:, 0:1], a["b_ck1"].rearrange("l e -> e l")),
            (b1[:, 1:2], a["b_cv1"].rearrange("l e -> e l")),
            (w2[:, 0, :], a["w_ck2"][0]), (w2[:, 1, :], a["w_cv2"][0]),
            
            (cosT[:, :], a["c_cosT"]), (sinT[:, :], a["c_sinT"]),
            (cosR[:, :, :], a["c_cosR"]), (sinR[:, :, :], a["c_sinR"]),
            (identb[:, :].bitcast(U16), a["c_identb"]), (causal[:, :].bitcast(U16), a["c_causal"]),
            (cmask[:, :, :].bitcast(U16), a["c_cmask"]), (rmask[:, :, :].bitcast(U16), a["c_rmask"]),
            (perm[:, :], a["c_perm"]), (hsum[:, :], a["c_hsum"]), (ovl[:, :], a["c_ovl"]),
            (jidx[:, :], a["c_jidx"]), (bonus[:, :], a["c_bonus"]), (anyok[:, :], a["c_anyok"]),
            (onesC[:, :], a["c_ones"]),
            (pmod[:, :], a["c_pmod"]),
        ]
        pt = a["page_table"]
        idx_loads = [(pidx[n * 64:(n + 1) * 64, r:r + 1], pt[2 * r + n, :].unsqueeze(1).to_broadcast([NPG, 8]).unsqueeze(2)) for n in range(2) for r in range(DB // 2)]
        quad_pt = pt.rearrange("b (h p) -> p (b h)", h=2)
        idx_loads += [(pidx[n * 32:(n + 1) * 32, DB // 2:], quad_pt[n:n + 1, :].to_broadcast([32, 2 * DB])) for n in range(4)]
        ALL_CONST = 16 * len(consts)

        firsts = [(ident[:, :], a["c_ident"]), (mhalf[:, :], a["c_mhalf"]), (gmix[:, :], a["g_mix"].rearrange("l (k p) -> p (l k)", p=P))]

        def more_blocks(eng):
            n = 2 * NUSUAL - NE
            return eng.value_load(eid[0:1, n:n + 1], min_val=0, max_val=NE)

        def loads(p, per):
            late = max(0, p - NE // 2 + 2) // 2
            return 16 * per * (p // 2 + 1 + late)

        @block.sync
        def _(sp):
            for i in range(QT):
                sp.dma_start(h[:, i, :], a["x_prompt"][0, i * P:(i + 1) * P, :]).then_inc(s_x, 16)
            sp.dma_start(h[0:NS_TOK, QT, :], a["x_sample"].rearrange("b t d -> (b t) d")).then_inc(s_x, 16)
            sp.wait_ge(s_x, 16 * NT)
            sp.dma_start(wkv, w_in_v[:, :, KV0:KV0 + KVN]).then_inc(s_wkv, 16)
            for c in range(CC):
                for half in (1, 0):
                    n = 2 * c + 1 - half
                    if n >= 4:
                        take(sp, J_GLU + n - 4)
                    col = U0 + half * C + c * P
                    sp.dma_start(wring[n % 4], w_in_v[:, :, col:col + P]).then_inc(s_wring[n % 4], 16)
            take(sp, J_NORM + KD - 1)
            sp.dma_start(wdr, a["w_dw"][0]).then_inc(s_cst, 16)
            sp.dma_start(cst[0:120, :, :], a["state_conv"][0].rearrange("(a b) k c -> (b k) a c", a=2)).then_inc(s_cst, 16)
            with sp.Fori(0, 4) as it:
                for u in range(4):
                    take(sp, J_MG - 4 + u, it=it, per=4)
                    sp.dma_start(wring[u], w_in_v[:, :, bass.ds(it * (4 * P) + (MG0 + u * P), P)]).then_inc(s_wring[u], 16)
            take(sp, J_MG + 2 * KD - 1)
            sp.wait_ge(s_cso, 16 * (1 + DB))
            sp.wait_ge(s_anew, CC)
            sp.wait_ge(s_rope, NT)
            for name, j0 in (("w_ck1", J_CMP), ("w_cv1", J_CMPV)):
                if j0 == J_CMPV:
                    take(sp, J_CMP + DB + 2)
                for r in range(2):
                    sp.dma_start(w1[:, :, r * HD:(r + 1) * HD],
                                 a[name][0, r * 16:(r + 1) * 16].rearrange("(j q) d e -> (q d) j e", q=2)).then_inc(s_w1, 16)
            wqv = a["w_in"][0, :, Q0:Q0 + C].rearrange("(k p) (g c e) -> p k g c e", p=P, g=NKV, c=HPG)
            take(sp, J_CMPV + DB + 2)
            with sp.Fori(0, 2) as it:
                for u in range(2):
                    take(sp, J_Q + (u - 2) * Q_PER, it=it, per=2 * Q_PER)
                    for g in range(NKV):
                        sp.dma_start(wq[u][:, :, g * HD:(g + 1) * HD], wqv[:, :, g, bass.ds(it * 2 + u, 1), :].rearrange("p k c e -> p k (c e)")).then_inc(s_wq[u], 16)

            skw, svw = (a[n][0].rearrange("b (k r) g d -> r b k (g d)", r=P) for n in ("state_k_win", "state_v_win"))

            def others(it):
                take(sp, J_S - 10, it=it, per=S_PER)
                for b in range(2):
                    sp.dma_start(kwraw[:, b, :, :], skw[:, bass.ds(it * 2 + b, 1), :, :].rearrange("r b k c -> r (b k) c")).then_inc(s_kw, 16)
                take(sp, J_S - 1, it=it, per=S_PER)
                for b in range(2):
                    new = bass.ds(it * 2 + b, 1)
                    sp.dma_start(vst[0:DS, b, 0, :], o["v_sel_s"][0, new].rearrange("b t g d -> (b t) (g d)")).then_inc(s_vw, 16)
                    sp.dma_start(vst[0:DS, b, 1, :], o["v_win_s"][0, new, WIN - DS:WIN].rearrange("b t g d -> (b t) (g d)")).then_inc(s_vw, 16)
                    sp.dma_start(vwin[:, b, :, :], svw[:, bass.ds(it * 2 + b, 1), :, :].rearrange("r b k c -> r (b k) c")).then_inc(s_vw, 16)

            sp.dma_start(a["xscratch"], a["c_zero"].to_broadcast([NBLK * BR, D])).then_inc(s_zero, 16)
            sp.dma_start(a["yscratch"][NUSUAL * P:, :], a["c_zero"].to_broadcast([(NPAIR - NUSUAL) * P, D])).then_inc(s_zero, 16)
            sp.wait_ge(s_kvout, 16 * N_KVOUT)
            take(sp, J_S - 1)
            sp.dma_start(wco, a["w_conv_out"][0].rearrange("(c p) n -> p c n", p=P)).then_inc(s_wout, 16)
            with sp.Fori(0, DB // 2) as it:
                others(it)
            sp.wait_ge(s_conv, 2 * CC * TAPS)
            for c in range(HPG):
                for g in range(NKV):
                    r0 = (g * HPG + c) * HD
                    sp.dma_start(wno[c][g * HD:(g + 1) * HD, :], a["w_nsa_out"][0, r0:r0 + HD, :]).then_inc(s_wout, 16)
            take(sp, J_LN - 1)
            sp.dma_start(wo, a["w_o"][0].rearrange("(k p) n -> p k n", p=P)).then_inc(s_wo, 16)
            sp.dma_start(gfin, a["g_final"].rearrange("(o n) -> o n", o=1).to_broadcast([P, D])).then_inc(s_gfin, 16)
            sp.wait_ge(s_merged, KD)
            with nc.allow_non_contiguous_dma(reason="a few columns"):
                sp.dma_start(wr[:, :, 0:NG], a["w_rg"][0].rearrange("(k p) n -> p k n", p=P)).then_inc(s_wr, 16)
            sp.dma_start(wr[:, :, NG:NR], a["w_re"][0].rearrange("(k p) n -> p k n", p=P)).then_inc(s_wr, 16)
            sp.dma_start(brow[:, 0:NG], a["b_rg"].to_broadcast([P, NG])).then_inc(s_wr, 16)
            sp.dma_start(brow[:, NG:NR], a["b_re"].to_broadcast([P, NE])).then_inc(s_wr, 16)
            sp.dma_start(tri, a["c_tri"]).then_inc(s_wr, 16)
            sp.dma_start(cidx, a["c_idx"].to_broadcast([P, N_CIDX])).then_inc(s_wr, 16)
            def pair_gates_ups(s, experts):
                for w, name in ((wgate, "w_gate"), (wup, "w_up")):
                    for at, e in experts:
                        sp.dma_start(w[s][:, at, :, :].rearrange("p e k f -> p e (k f)"), a[name][0, e].rearrange("e (p k) f -> p e (k f)", p=P)).then_inc(s_we[s], 16)

            def pair_downs(s, experts):
                for at, e in experts:
                    sp.dma_start(wdn[s][:, at, :], a["w_down"][0, e].rearrange("e f n -> f e n")).then_inc(s_wd[s], 16)

            BOTH = slice(0, 2)
            one_by_one = lambda experts: [(slice(u, u + 1), e) for u, e in enumerate(experts)]

            def load_rows(at, s):
                sp.dma_start(xe[s], a["xscratch"][at, :]).then_inc(s_xe[s], 16)

            def pair_weights(s, experts, j=None, rows=None, it=None):
                if j is not None:
                    take(sp, j + 1, it=it, per=2 * E_PER)
                    load_rows(*rows)
                pair_gates_ups(s, experts)
                if j is not None:
                    take(sp, j + 3, it=it, per=2 * E_PER)
                pair_downs(s, experts)

            take(sp, J_WO + NT - 1)
            for p in range(2):
                pair_weights(p, [(BOTH, slice(2 * p, 2 * p + 2))])
            sp.wait_ge(s_scat, 16 * 2 * NT)
            for p in range(3):
                load_rows(slice(p * P, (p + 1) * P), p)
            trips = NE // 8 - 1
            with sp.Fori(0, trips) as it:
                for p in range(4):
                    pair_weights(p % 2, [(BOTH, bass.ds(it * 8 + (2 * p + 4), 2))], J_MOE + 4 * p,
                                 (bass.ds(it * (4 * P) + (p + 3) * P, P), (p + 3) % 4), it)
            for p in range(4 * trips + 2, NE // 2):
                pair_weights(p % 2, [(BOTH, slice(2 * p, 2 * p + 2))], J_MOE + 4 * (p - 2),
                             (slice((p + 1) * P, (p + 2) * P), (p + 1) % 4))
            sp.wait_ge(s_eid, 2)
            def over_pair(s, at, j, rows, it=None):
                used = sp.value_load(eid[0:1, at(0)], min_val=0, max_val=NE)
                experts = [bass.ds(sp.value_load(eid[0:1, at(N_OVER + u)], min_val=0, max_val=NE - 1), 1) for u in range(2)]
                take(sp, j + 1, it=it, per=2 * E_PER)
                if rows is not None:
                    load_rows(*rows)
                sp.nop(nofuse=True)
                with sp.If(used < NE):
                    pair_gates_ups(s, one_by_one(experts))
                with sp.Else():
                    sp.sem_inc(s_we[s], 64)
                take(sp, j + 3, it=it, per=2 * E_PER)
                sp.nop(nofuse=True)
                with sp.If(used < NE):
                    pair_downs(s, one_by_one(experts))
                with sp.Else():
                    sp.sem_inc(s_wd[s], 32)

            for q in range(NE // 2, NUSUAL):
                p = q - NE // 2
                over_pair(p % 2, lambda x: slice(2 * p + x, 2 * p + x + 1), J_MOE + 4 * (q - 2),
                          (slice((q + 1) * P, (q + 2) * P), (q + 1) % 4) if q + 1 < NUSUAL else None)
            more = more_blocks(sp)
            with sp.If(more < NE):
                for q in range(NUSUAL, NPAIR):
                    experts = [bass.ds(sp.value_load(eid[0:1, n:n + 1], min_val=0, max_val=NE - 1), 1)
                               for n in range(N_OVER + 2 * q - NE, N_OVER + 2 * q - NE + 2)]
                    pair_weights(q % 2, one_by_one(experts), J_MOE + 4 * (q - 2), (slice(q * P, (q + 1) * P), q % 4))
            for i in range(NT):
                sp.wait_ge(s_final, i + 1)
                if i < QT:
                    sp.dma_start(o["y_prompt"][0, i * P:(i + 1) * P, :], h[:, i, :]).then_inc(s_out, 16)
                else:
                    sp.dma_start(o["y_sample"].rearrange("b t d -> (b t) d"), h[0:NS_TOK, i, :]).then_inc(s_out, 16)
            sp.wait_ge(s_out, 16 * NT)
            sp.wait_ge(s_kvout, 16 * N_KVOUT)
            sp.wait_ge(s_cso, 16 * (1 + DB))
            sp.wait_ge(s_kcout, 32)
            sp.wait_ge(s_moved, 16 * 3)

        order = [("S", 0, 0), ("S", 0, 1), ("C", 0, 0)]
        for qt in range(1, QT):
            order += [("S", qt, 0), ("T", qt - 1, 0), ("S", qt, 1), ("T", qt - 1, 1), ("C", qt, 0), ("TC", qt - 1, 0), ("O", qt - 1, 0)]
        order += [("T", QT - 1, 0), ("T", QT - 1, 1), ("TC", QT - 1, 0), ("O", QT - 1, 0), ("OT", 0, 0), ("OT", 1, 0)]
        assert len(order) + 2 == Q_PER
        job_of = {x: J_Q + 2 + n for n, x in enumerate(order)}
        score_jobs = [x for x in order if x[0] in "SC" and len(x[0]) == 1]
        N_SCORE = len(score_jobs)

        def on(t, i):
            return slice(0, TS[i])

        def scales(pool, st, n):
            pool.wait_ge(s_sq, NT * (n + 1))
            st.do(nc.gpsimd.tensor_scalar(rs[:, n, 0:NT], ss[:, n, 0:NT], 1.0 / D, EPS, ALU.mult, ALU.add))
            nc.gpsimd.tensor_tensor(rs[:, n, 0:NT], rs[:, n, 0:NT], mhalf[:, 0:NT], ALU.pow).then_inc(s_pow, 1)

        def spread(copy, how, j, u, it):
            for q in range(2):
                for g in range(NKV):
                    v = slot(j)[g * HD:(g + 1) * HD, :].rearrange("p (k q s) -> p k q s", q=2, s=P)[:, :, q, :]
                    k0 = (u % 2) * (KD // 2)
                    last = copy(XT[q * HD:(q + 1) * HD, g, k0:k0 + KD // 2, bass.ds(it * (2 * P) + (u // 2) * P, P)], v, *how)
            return last

        def spread_own(copy, how, j):
            for q in range(2):
                for g in range(NKV):
                    v = slot(j)[g * HD:(g + 1) * HD, 0:512].rearrange("p (k q s) -> p k q s", q=2, s=STR_P)[:, :, q, :]
                    last = copy(XT[q * HD:(q + 1) * HD, g, :, STR_S:STR], v, *how)
            return last

        @block.gpsimd
        def _(pool):
            st = Steps(pool, s_pool)
            nc.gpsimd.memset(ss[:, :, :], 1.0).then_inc(s_pads, 1)
            nc.gpsimd.memset(aP[:, :, 0:PAD], 0.0).then_inc(s_pads, 1)
            nc.gpsimd.memset(pre, 0.0).then_inc(s_pads, 1)
            pool.wait_ge(s_first, 16 * len(firsts))
            scales(pool, st, 0)
            pool.wait_ge(s_const, ALL_CONST)
            for i in range(NT):
                result_of(pool, J_KV + i)
                r = on(h, i)
                x = kv[r, i, 2 * P:6 * P].rearrange("p (s x) -> p s x", x=2 * P)[:, :, 0:P].rearrange("p s (g h e) -> p s g h e", g=NKV, h=2)
                y = rot[r, i, :, :].rearrange("p s (g h e) -> p s g h e", g=NKV, h=2)
                full = [TS[i], 2, NKV, 32]
                for g in range(NKV):
                    co = cosR[r, i, :].unsqueeze(1).to_broadcast([TS[i], 2, 32])
                    si = sinR[r, i, :].unsqueeze(1).to_broadcast([TS[i], 2, 32])
                    t0, t1 = rtmp[r, 0, :, g, :], rtmp[r, 1, :, g, :]
                    nc.gpsimd.tensor_tensor(t0, x[:, :, g, 0, :], co, ALU.mult)
                    st.do(nc.gpsimd.tensor_tensor(t1, x[:, :, g, 1, :], si, ALU.mult))
                    st.do(nc.gpsimd.tensor_tensor(y[:, :, g, 0, :], t0, t1, ALU.subtract))
                    nc.gpsimd.tensor_tensor(t0, x[:, :, g, 1, :], co, ALU.mult)
                    st.do(nc.gpsimd.tensor_tensor(t1, x[:, :, g, 0, :], si, ALU.mult))
                    ins = nc.gpsimd.tensor_tensor(y[:, :, g, 1, :], t0, t1, ALU.add)
                    if g == 0:
                        st.do(ins)
                    else:
                        ins.then_inc(s_rope, 1)
            for c in range(CC):
                result_of(pool, J_GLU + 2 * c + 1)
                nc.gpsimd.tensor_copy(aS[:, c, :, PAD:], anew[:, c, :].rearrange("p (b t) -> p b t", t=DS)).then_inc(s_anew, 1)
            pool.wait_ge(s_rope, NT)
            tok = lambda t: t[0, 0].rearrange("(t p) g d -> p t (g d)", p=P)
            pool.dma_start(tok(o["k_cmp_p"]), kv[:, 0:QT, 0:P]).then_inc(s_kcout, 16)
            pool.dma_start(tok(o["v_cmp_p"]), kv[:, 0:QT, P:2 * P]).then_inc(s_kcout, 16)
            pool.dma_start(tok(o["k_sel_p"]), rot[:, 0:QT, 0, :]).then_inc(s_kvout, 16)
            pool.dma_start(tok(o["v_sel_p"]), kv[:, 0:QT, 3 * P:4 * P]).then_inc(s_kvout, 16)
            pool.dma_start(tok(o["k_win_p"]), rot[:, 0:QT, 1, :]).then_inc(s_kvout, 16)
            pool.dma_start(tok(o["v_win_p"]), kv[:, 0:QT, 5 * P:6 * P]).then_inc(s_kvout, 16)
            S64 = slice(0, NS_TOK)
            for name, src in (("k_cmp_s", kv[S64, QT, 0:P]), ("v_cmp_s", kv[S64, QT, P:2 * P]),
                              ("k_sel_s", rot[S64, QT, 0, :]), ("v_sel_s", kv[S64, QT, 3 * P:4 * P])):
                pool.dma_start(rows(o[name]), src).then_inc(s_kvout, 16)
            for b in range(DB):
                rb = slice(b * DS, (b + 1) * DS)
                pool.dma_start(o["k_win_s"][0, b, WIN - DS:WIN].rearrange("t g d -> t (g d)"), rot[rb, QT, 1, :]).then_inc(s_kvout, 16)
                pool.dma_start(o["v_win_s"][0, b, WIN - DS:WIN].rearrange("t g d -> t (g d)"), kv[rb, QT, 5 * P:6 * P]).then_inc(s_kvout, 16)
            for name, st_name in (("k_win_s", "state_k_win"), ("v_win_s", "state_v_win")):
                pool.dma_start(o[name][0, :, 0:WIN - DS].rearrange("b r g d -> b (r g d)"),
                               a[st_name][0, :, DS:WIN].rearrange("b r g d -> b (r g d)")).then_inc(s_moved, 16)
            pool.dma_start(o["conv_s"][0, :, 0:PAD - DS, :], a["state_conv"][0, :, DS:PAD, :]).then_inc(s_moved, 16)
            for dst, src in idx_loads:
                with nc.allow_non_contiguous_dma(reason="a few words"):
                    pool.dma_start(dst, src).then_inc(s_idx, 16)
            pool.wait_ge(s_idx, 16 * len(idx_loads))
            nc.gpsimd.tensor_scalar(gidx[:, 0:DB // 2], pidx[:, 0:DB // 2], float(PAGE // 16), pmod[:, 0:1], ALU.mult, ALU.add)
            st.do(nc.gpsimd.tensor_scalar(gidx[:, DB // 2:], pidx[:, DB // 2:], float(PAGE // 4), pmod[:, 1:2], ALU.mult, ALU.add))
            pool.wait_ge(s_gates, NT)
            pool.dma_start(a["gscratch"], gates[S64, QT, :]).then_inc(s_gsw, 16)
            pool.wait_ge(s_gsw, 16)
            for b in range(DB):
                src = a["gscratch"][b * DS:(b + 1) * DS, :].rearrange("t (h r) -> h t r", r=3)
                pool.dma_start(gS[(b % 2) * 64:(b % 2) * 64 + 64, b // 2, :], src).then_inc(s_gs, 16)
            result_of(pool, J_CSO)
            pool.dma_start(o["conv_p"][0, 0], cso[0:PAD, 0, :]).then_inc(s_cso, 16)
            for b in range(DB):
                pool.dma_start(o["conv_s"][0, b, PAD - DS:PAD, :], cso[b * DS:(b + 1) * DS, 1, :]).then_inc(s_cso, 16)
            take(pool, J_MG + 2 * KD - 1)
            pool.wait_ge(s_cso, 16 * (1 + DB))
            pool.wait_ge(s_kcout, 32)
            for name, own, j0 in (("cache_k_cmp", o["k_cmp_p"], J_CMP), ("cache_v_cmp", o["v_cmp_p"], J_CMPV)):
                for r in range(DB // 2):
                    if r >= 2:
                        take(pool, j0 + 2 * r - 3)
                    elif j0 == J_CMPV:
                        take(pool, J_CMP + DB - r)
                    pool.indirect_dma_start(raw[r % 2].rearrange("p a b -> p (a b)"), None, strides_of[name],
                                            bass.IndirectOffsetOnAxis(ap=gidx[:, r:r + 1], axis=0)).then_inc(s_raw[r % 2], 16)
                take(pool, j0 + 5)
                pool.dma_start(raw[0][0:STR_P, :, :], own[0, 0].rearrange("(s r) g d -> s r (g d)", r=16)).then_inc(s_raw[0], 16)

            def gather(name, dst, b, s):
                for half in range(2):
                    n = DB // 2 + 2 * b + half
                    pool.indirect_dma_start(dst[:, half * 4:(half + 1) * 4, :].rearrange("p a b -> p (a b)"), None, quads_of[name],
                                            bass.IndirectOffsetOnAxis(ap=gidx[:, n:n + 1], axis=0)).then_inc(s, 16)

            take(pool, J_CMPV + DB + 2)
            for b in range(2):
                gather("cache_k_sel", kraw[b], b, s_kin[b])
            take(pool, J_S - 1)
            result_of(pool, J_CMPV + DB + 3)
            nc.gpsimd.memset(pcn, 0.0)
            for pair in range(DB // 2):
                J = J_S + S_PER * pair
                take(pool, J + 4 - S_PER)
                for s in range(2):
                    for g in range(NKV):
                        src = qs[:, s, :, pair * 2 * DS:(pair + 1) * 2 * DS].rearrange("p c (b t) -> p b c t", b=2)
                        dst = qbd[:, s, :, g * HPG * DS:(g + 1) * HPG * DS].rearrange("p b (c t) -> p b c t", t=DS)
                        st.do(nc.gpsimd.tensor_scalar(dst, src, pmod[:, 2 + g:3 + g], None, ALU.mult))
                for s in range(2):
                    st.do(nc.gpsimd.tensor_copy(kdyn[:, :, s * DS:(s + 1) * DS], kT[:, s, SEQ + pair * 2 * DS:SEQ + (pair + 1) * 2 * DS].rearrange("p (b t) -> p b t", b=2)))
                nc.gpsimd.tensor_copy(kdyn[:, :, 2 * DS:2 * DS + HD], kcT[:, pair * 2 * HD:(pair + 1) * 2 * HD].rearrange("p (b n) -> p b n", b=2)).then_inc(s_qbd, 1)
                take(pool, J - 1, J - 2)
                nc.gpsimd.tensor_copy(vst[:, :, 2, :], vcS[:, pair * 2:(pair + 1) * 2, :]).then_inc(s_vst, 1)
                for b in range(2):
                    gather("cache_v_sel", vsel[b], 2 * pair + b, s_vin[b])
                if pair < DB // 2 - 1:
                    for b in range(2):
                        take(pool, J + b)
                        gather("cache_k_sel", kraw[b], 2 * pair + 2 + b, s_kin[b])
            scales(pool, st, 1)
            pool.wait_ge(s_zero, 32)
            pool.wait_ge(s_dest, 1)
            pool.wait_ge(s_xs, 2 * NT)
            for i in range(NT):
                for k in range(2):
                    pool.indirect_dma_start(a["xscratch"], bass.IndirectOffsetOnAxis(ap=dest[on(h, i), i, k:k + 1], axis=0),
                                            xs2[on(h, i), i, :], None).then_inc(s_scat, 16)
            pool.wait_ge(s_eid, 2)
            more = more_blocks(pool)
            with pool.If(more < NE):
                for s in range(2):
                    pool.wait_ge(s_ye[s], 16 * ((NPAIR + 1 - s) // 2))
            for s in range(2):
                pool.wait_ge(s_ye[s], 16 * ((NUSUAL + 1 - s) // 2))
            for i in range(NT):
                for k in range(2):
                    pool.indirect_dma_start(got[k][on(h, i), i, :], None, a["yscratch"],
                                            bass.IndirectOffsetOnAxis(ap=dest[on(h, i), i, k:k + 1], axis=0)).then_inc(s_got[i], 16)
            scales(pool, st, 2)

        @block.scalar
        def _(act):
            for dst, src in firsts:
                with nc.allow_non_contiguous_dma(reason="small vectors, once"):
                    act.dma_start(dst, src).then_inc(s_first, 16)
            act.wait_ge(s_x, 16 * NT)
            act.wait_ge(s_pads, 1)
            for i in range(NT):
                nc.scalar.activation(xs[on(xs, i), i, :], h[on(h, i), i, :], ACT.Square, accum_out=ss[on(ss, i), 0, i:i + 1]).then_inc(s_sq, 1)
            for k in range(1, KD, 2):
                take(act, J_NORM + k)
                give(nc.scalar.activation(xT[:, k, :], slot(J_NORM + k)[:, 0:T], ACT.Copy, scale=gmix[:, k:k + 1]), J_NORM + k)
            for dst, src in consts:
                with nc.allow_non_contiguous_dma(reason="small vectors, once"):
                    act.dma_start(dst, src).then_inc(s_const, 16)
            for i in range(NT):
                take(act, J_KV + i)
                give(nc.scalar.activation(kv[on(kv, i), i, :], slot(J_KV + i)[on(kv, i), 0:KVN], ACT.Copy), J_KV + i)
            for i in range(NT):
                result_of(act, J_KV + i)
                nc.scalar.activation(gates[on(kv, i), i, :], kv[on(kv, i), i, 6 * P:KVN], ACT.Sigmoid).then_inc(s_gates, 1)
            for c in range(CC):
                take(act, J_GLU + 2 * c)
                if c >= 2:
                    result_of(act, J_GLU + 2 * c - 3)
                give(nc.scalar.activation(sg[c % 2], slot(J_GLU + 2 * c)[:, 0:T], ACT.Sigmoid), J_GLU + 2 * c)
            take(act, J_CSO)
            nc.scalar.activation(cso[0:PAD, 0, :], slot(J_CSO)[0:PAD, 0:C], ACT.Copy)
            give(nc.scalar.activation(cso[0:NS_TOK, 1, :], slot(J_CSO)[0:NS_TOK, C:2 * C], ACT.Copy), J_CSO)
            with act.Fori(0, 4) as it:
                for u in range(4):
                    take(act, J_MG + u, it=it, per=4)
                    give(nc.scalar.activation(mgT[:, bass.ds(it * 4 + u, 1), :].rearrange("p a b -> p (a b)"), slot(J_MG + u)[:, 0:T], ACT.Sigmoid), J_MG + u)
            for s, j0 in enumerate((J_CMP, J_CMPV)):
                with act.Fori(0, 2) as it:
                    for u in (0, 2):
                        take(act, j0 + u, it=it, per=4)
                        give(spread(nc.scalar.activation, (ACT.Copy,), j0 + u, u, it), j0 + u)
                take(act, j0 + DB)
                give(spread_own(nc.scalar.activation, (ACT.Copy,), j0 + DB), j0 + DB)
                take(act, j0 + DB + 1)
                nc.scalar.activation(upper[:, :, 0:STR_S], slot(j0 + DB + 1)[HD:P, :].rearrange("p (g n) -> p g n", g=NKV), ACT.Copy).then_inc(s_upper, 1)
                take(act, j0 + DB + 2)
                nc.scalar.activation(upper[:, :, STR_S:STR], slot(j0 + DB + 2)[HD:P, 0:2 * STR_P].rearrange("p (g n) -> p g n", g=NKV), ACT.Copy).then_inc(s_upper, 1)
                result_of(act, j0 + DB + 1)
                result_of(act, j0 + DB + 2)
                nc.scalar.activation(upper, pre, ACT.Silu).then_inc(s_silu, 1)
            take(act, J_CMPV + DB + 3)
            give(nc.scalar.activation(vcS[:, :, :].rearrange("p b n -> p (b n)"), slot(J_CMPV + DB + 3)[0:HD, :], ACT.Copy), J_CMPV + DB + 3)
            with act.Fori(0, HPG) as it:
                take(act, J_Q, it=it, per=Q_PER)
                nc.scalar.activation(qT, slot(J_Q)[:, 0:T], ACT.Copy, scale=HD ** -0.5)
                give(nc.scalar.activation(qs[:, 0, bass.ds(it, 1), :].rearrange("p a b -> p (a b)"), slot(J_Q)[:, SEQ:T], ACT.Copy, scale=HD ** -0.5), J_Q)
                for kind, qt, g in order:
                    j = job_of[(kind, qt, g)]
                    nk = (qt + 1) * P
                    if kind == "S":
                        n = score_jobs.index((kind, qt, g))
                        take(act, j, it=it, per=Q_PER)
                        act.wait_ge(s_max, it * N_SCORE + (n + 1))
                        for br in range(2):
                            last = nc.scalar.activation(Pb[(2 * qt + g) % 4][:, br, 0:nk], slot(j)[:, br * 512:br * 512 + nk], ACT.Exp,
                                                        bias=smx[:, n, br:br + 1], accum_out=sms[:, qt, g, br + 1:br + 2])
                        give(last, j)
                    if kind == "C":
                        n = score_jobs.index((kind, qt, g))
                        take(act, j, it=it, per=Q_PER)
                        act.wait_ge(s_max, it * N_SCORE + (n + 1))
                        for g2 in range(NKV):
                            last = nc.scalar.activation(Pc[qt % 2][:, g2, 0:NCP], slot(j)[:, g2 * 512:g2 * 512 + NCP], ACT.Exp,
                                                        bias=smx[:, n, g2:g2 + 1], accum_out=sms[:, qt, g2, 0:1])
                        give(last, j)
                    if kind == "T" and g == 1:
                        take(act, j, *([job_of[("O", qt - 1, 0)]] if qt else []), it=it, per=Q_PER)
                        give(nc.scalar.activation(PT[1][:, :, 0:nk], slot(j).rearrange("p (b n) -> p b n", b=2)[:, :, 0:nk], ACT.Copy), j)
                    if kind == "TC":
                        take(act, j, it=it, per=Q_PER)
                        give(nc.scalar.activation(PcT[0:NCP, :, :].rearrange("p a b -> p (a b)"), slot(j)[0:NCP, 0:2 * P], ACT.Copy), j)
                    if kind == "OT":
                        take(act, j, it=it, per=Q_PER)
                        give(nc.scalar.activation(oT[:, bass.ds(it, 1), qt * 2 * P:(qt + 1) * 2 * P].rearrange("p a b -> p (a b)"), slot(j)[:, 0:2 * P], ACT.Copy), j)
            with act.Fori(0, DB // 2) as it:
                J = J_S
                take(act, J, it=it, per=S_PER)
                give(nc.scalar.activation(ksT[0], slot(J), ACT.Copy), J)
                take(act, J + 2, it=it, per=S_PER)
                give(nc.scalar.activation(kwT.rearrange("p b n -> p (b n)"), slot(J + 2), ACT.Copy), J + 2)
                take(act, J + 3, it=it, per=S_PER)
                act.wait_ge(s_snew, it + 1)
                nc.scalar.activation(Ps[:, CMP0:PW], slot(J + 3)[:, 528:528 + NCS], ACT.Exp, bias=sv[:, 0:1], accum_out=sv[:, 24:25]).then_inc(s_expc, 1)
                give(nc.scalar.activation(Ps[:, PAST:PAST + WIN], slot(J + 3)[:, 0:WIN], ACT.Exp, bias=sv[:, 3:4], accum_out=sv[:, 11:12]), J + 3)
                nc.scalar.activation(Ps[:, CMP0 - DS:CMP0], snew[:, DS:2 * DS], ACT.Exp, bias=sv[:, 3:4], accum_out=sv[:, 12:13])
                take(act, J + 5, it=it, per=S_PER)
                give(nc.scalar.activation(PTn[0:NCS, 2, :], slot(J + 5)[0:NCS, 0:P], ACT.Copy), J + 5)
                act.wait_ge(s_maxs, it + 1)
                give(nc.scalar.activation(Ps[:, 0:PAST], slot(J + 4), ACT.Exp, bias=sv[:, 6:7], accum_out=sv[:, 9:10]), J + 4)
                nc.scalar.activation(Ps[:, CMP0 - 2 * DS:CMP0 - DS], snew[:, 0:DS], ACT.Exp, bias=sv[:, 6:7], accum_out=sv[:, 10:11]).then_inc(s_exps, 1)
                take(act, J + 9, it=it, per=S_PER)
                nc.scalar.activation(PTs[:, 8:12, :].rearrange("p a b -> p (a b)"), slot(J + 9)[:, 0:512], ACT.Copy)
                nc.scalar.activation(PTn[0:DS, 0:2, :].rearrange("p a b -> p (a b)"), slot(J + 9)[0:DS, 512:768], ACT.Copy)
                give(nc.scalar.activation(PTn[0:NCS, 2, :], slot(J + 9)[0:NCS, 768:896], ACT.Copy), J + 9)
                take(act, J + 11, it=it, per=S_PER)
                for g in range(NKV):
                    r = slice(g * HD, (g + 1) * HD)
                    last = nc.scalar.activation(oT[r, :, bass.ds(it * (2 * DS) + (SEQ + DS), DS)],
                                                slot(J + 11)[r, g * 32:(g + 1) * 32].rearrange("p (c t) -> p c t", t=DS), ACT.Copy)
                give(last, J + 11)
            for c in range(CC):
                if c < CC - 1:
                    act.wait_ge(s_xc, c + 1)
                else:
                    result_of(act, J_LN)
                nc.scalar.activation(sq[:, c, :], cv[:, c, :], ACT.Square).then_inc(s_sqd, 1)
            result_of(act, J_LN + 1)
            nc.scalar.activation(rstd, rstd, ACT.Sqrt).then_inc(s_var, 1)
            for c in range(CC):
                act.wait_ge(s_cn, c + 1)
                nc.scalar.activation(cv[:, c, :], cv[:, c, :], ACT.Silu, scale=cng[:, c:c + 1], bias=cnb[:, c:c + 1]).then_inc(s_silc, 1)
            for i in range(NT):
                result_of(act, J_WO + i)
                nc.scalar.activation(xs2[on(h, i), i, :], h[on(h, i), i, :], ACT.Square, accum_out=ss[on(h, i), 1, i:i + 1]).then_inc(s_sq, 1)
            for k in range(1, KD, 2):
                take(act, J_N2 + k)
                give(nc.scalar.activation(xT[:, k, :], slot(J_N2 + k)[:, 0:T], ACT.Copy, scale=gffn[:, k:k + 1]), J_N2 + k)
            act.wait_ge(s_sub, 1)
            nc.scalar.activation(rt[:, 5, 0:NT * NG], rt[:, 5, 0:NT * NG], ACT.Exp).then_inc(s_ex, 1)
            act.wait_ge(s_sub, 2)
            nc.scalar.activation(rt[:, 12, 0:NT], rt[:, 12, 0:NT], ACT.Exp).then_inc(s_ex, 1)
            def activate(j, s, it=None):
                take(act, j + 1, it=it, per=E_PER)
                result_of(act, j + 1 - 8, it=it, per=E_PER)
                nc.scalar.activation(sil[s], slot(j + 1)[:, 0:P], ACT.Silu).then_inc(s_sil, 1)

            def results(j, s, stored, rows, it=None):
                act.wait_ge(s_ye[s], stored) if stored is not None else None
                for half in range(2):
                    take(act, j + 2 + half, it=it, per=E_PER)
                    give(nc.scalar.activation(ye[s][:, half * 512:(half + 1) * 512], slot(j + 2 + half)[:, 0:512], ACT.Copy), j + 2 + half)
                result_of(act, j + 2, j + 3, it=it, per=E_PER)
                act.dma_start(a["yscratch"][rows, :], ye[s]).then_inc(s_ye[s], 16)

            def pair(p):
                activate(J_MOE + 4 * p, p % 2)
                results(J_MOE + 4 * p, p % 2, 16 * (p // 2) if p > 1 else None, slice(p * P, (p + 1) * P))

            for p in range(2):
                pair(p)
            loops = (NUSUAL - 2) // 2
            with act.Fori(0, loops) as it:
                for u in range(2):
                    activate(J_MOE + 4 * (u + 2), u, it)
                    results(J_MOE + 4 * (u + 2), u, it * 16 + 16, bass.ds(it * (2 * P) + (u + 2) * P, P), it)
            for p in range(2 + 2 * loops, NUSUAL):
                pair(p)
            act.wait_ge(s_eid, 2)
            act.wait_ge(s_zero, 32)
            more = more_blocks(act)
            with act.If(more < NE):
                for p in range(NUSUAL, NPAIR):
                    pair(p)
            for i in range(NT):
                act.wait_ge(s_hy, i + 1)
                nc.scalar.activation(got[0][on(h, i), i, :], h[on(h, i), i, :], ACT.Square, accum_out=ss[on(h, i), 2, i:i + 1]).then_inc(s_sq, 1)

        @block.vector
        def _(dve):
            st = Steps(dve, s_dve)
            V = nc.vector
            dve.wait_ge(s_pow, 1)
            for i in range(NT):
                r = on(h, i)
                V.tensor_scalar(xs[r, i, :], h[r, i, :], rs[r, 0, i:i + 1], None, ALU.mult).then_inc(s_xs, 1)
            for k in range(0, KD, 2):
                take(dve, J_NORM + k)
                give(V.tensor_scalar(xT[:, k, :], slot(J_NORM + k)[:, 0:T], gmix[:, k:k + 1], None, ALU.mult), J_NORM + k)
            dve.wait_ge(s_pads, 2)
            for c in range(CC):
                j = J_GLU + 2 * c + 1
                take(dve, j)
                result_of(dve, j - 1)
                V.tensor_tensor(aP[:, c, PAD:], slot(j)[:, 0:SEQ], sg[c % 2][:, 0:SEQ], ALU.mult)
                give(V.tensor_tensor(anew[:, c, :], slot(j)[:, SEQ:T], sg[c % 2][:, SEQ:T], ALU.mult), j)
            for s in range(2):
                take(dve, J_KT + s)
                give(V.tensor_copy(kT[:, s, :], slot(J_KT + s)[:, 0:T]), J_KT + s)
            take(dve, J_CST)
            for c in range(CC):
                at = (c // 2) * 512 + (c % 2) * 240
                last = V.tensor_copy(aS[:, c, :, 0:PAD], slot(J_CST)[:, at:at + DB * PAD].rearrange("p (b k) -> p b k", k=PAD))
            give(last, J_CST)
            take(dve, J_WDW)
            give(V.tensor_copy(wdw[:, :, :].rearrange("p c k -> p (c k)"), slot(J_WDW)[:, 0:CC * TAPS]), J_WDW)
            dve.wait_ge(s_gates, NT)
            gc = gates[:, 0, :].rearrange("p (h r) -> p h r", r=3)[:, :, 0]
            V.tensor_scalar(gc, gc, anyok[:, 0:1], None, ALU.mult).then_inc(s_anyok, 1)
            result_of(dve, J_CST, J_WDW)
            dve.wait_ge(s_anew, CC)
            for c in range(CC):
                for dst, src in ((cv[:, c, 0:SEQ], aP[:, c, 0:SEQ]),
                                 (cv[:, c, SEQ:T].rearrange("p (b t) -> p b t", t=DS), aS[:, c, :, 0:DS])):
                    V.tensor_scalar(dst, src, wdw[:, c, 0:1], bdw[:, c:c + 1], ALU.mult, ALU.add).then_inc(s_conv, 1)
            with dve.Fori(1, TAPS) as k:
                for c in range(CC):
                    for n, (dst, src) in enumerate(((cv[:, c, 0:SEQ], aP[:, c, bass.ds(k, SEQ)]),
                                                    (cv[:, c, SEQ:T].rearrange("p (b t) -> p b t", t=DS), aS[:, c, :, bass.ds(k, DS)]))):
                        dve.wait_ge(s_conv, k * (2 * CC) + (2 * c + n - 2 * CC + 1))
                        V.scalar_tensor_tensor(dst, src, wdw[:, c, bass.ds(k, 1)], dst, ALU.mult, ALU.add).then_inc(s_conv, 1)
            for s, j0 in enumerate((J_CMP, J_CMPV)):
                with dve.Fori(0, 2) as it:
                    for u in (1, 3):
                        take(dve, j0 + u, it=it, per=4)
                        give(spread(V.tensor_copy, (), j0 + u, u, it), j0 + u)
                dve.wait_ge(s_pads, 3)
                take(dve, j0 + DB + 1)
                dve.wait_ge(s_upper, 2 * s + 1)
                for g in range(NKV):
                    lo = slot(j0 + DB + 1)[0:HD, g * 512:(g + 1) * 512].rearrange("p (b n) -> p b n", b=DB)
                    last = V.scalar_tensor_tensor(pre[:, g, 0:STR_S].rearrange("p (b n) -> p b n", b=DB)[:, :, 0:NCS], lo[:, :, 0:NCS], b1[:, s:s + 1],
                                                  upper[:, g, 0:STR_S].rearrange("p (b n) -> p b n", b=DB)[:, :, 1:NCS + 1], ALU.add, ALU.add)
                give(last, j0 + DB + 1)
                take(dve, j0 + DB + 2)
                dve.wait_ge(s_upper, 2 * s + 2)
                for g in range(NKV):
                    last = V.scalar_tensor_tensor(pre[:, g, STR_S:STR_S + NCP], slot(j0 + DB + 2)[0:HD, g * STR_P:g * STR_P + NCP], b1[:, s:s + 1],
                                                  upper[:, g, STR_S + 1:STR_S + 1 + NCP], ALU.add, ALU.add)
                give(last, j0 + DB + 2)
                if s == 0:
                    take(dve, j0 + DB + 3)
                    give(V.tensor_copy(kcT[:, :], slot(j0 + DB + 3)[:, 0:STR]), j0 + DB + 3)
            take(dve, J_CMPV + DB + 4)
            give(V.tensor_copy(vcP[:, :], slot(J_CMPV + DB + 4)[0:32, 0:P]), J_CMPV + DB + 4)
            N_STEP = 29
            with dve.Fori(0, HPG) as it:
                st.begin(it, N_STEP)
                take(dve, J_Q + 1, it=it, per=Q_PER)
                result_of(dve, J_Q, it=it, per=Q_PER)
                give(V.tensor_tensor(qtmp[:, 0, :], slot(J_Q + 1)[:, 0:T], sinT[:, :], ALU.mult), J_Q + 1)
                st.do(V.tensor_tensor(qtmp[:, 1, :], qT, cosT[:, :], ALU.mult))
                result_of(dve, J_Q + 1, it=it, per=Q_PER)
                V.tensor_tensor(qrot, qtmp[:, 0, :], qtmp[:, 1, :], ALU.add).then_inc(s_qrot, 1)
                V.tensor_tensor(qs[:, 1, bass.ds(it, 1), :].rearrange("p a b -> p (a b)"), qtmp[:, 0, SEQ:T], qtmp[:, 1, SEQ:T], ALU.add)
                for kind, qt, g in order:
                    j = job_of[(kind, qt, g)]
                    nk = (qt + 1) * P
                    if kind in ("S", "C"):
                        n = score_jobs.index((kind, qt, g))
                        take(dve, j, it=it, per=Q_PER)
                        w = nk if kind == "S" else NCP
                        V.tensor_reduce(smx[:, n, :], slot(j).rearrange("p (b n) -> p b n", b=2)[:, :, 0:w], AX.X, ALU.max, negate=True).then_inc(s_max, 1)
                    if kind == "T" and g == 0:
                        take(dve, j, it=it, per=Q_PER)
                        give(V.tensor_copy(PT[0][:, :, 0:nk], slot(j).rearrange("p (b n) -> p b n", b=2)[:, :, 0:nk]), j)
                    if kind == "O":
                        result_of(dve, *[job_of[x] for x in (("S", qt, 0), ("S", qt, 1), ("C", qt, 0))], it=it, per=Q_PER)
                        st.do(V.reciprocal(sms[:, qt, :, :], sms[:, qt, :, :]))
                        gv = gates[:, qt, :].rearrange("p (g c r) -> p g c r", g=NKV, c=HPG)[:, :, bass.ds(it, 1), :].rearrange("p g c r -> p g (c r)")
                        st.do(V.tensor_tensor(coef, sms[:, qt, :, :], gv, ALU.mult))
                        take(dve, j, it=it, per=Q_PER)
                        for g2 in range(NKV):
                            at = otok[:, qt, g2 * HD:(g2 + 1) * HD]
                            cc = lambda b: coef[:, g2, b:b + 1]
                            st.do(V.tensor_scalar(at, slot(j)[:, 128 + g2 * HD:128 + (g2 + 1) * HD], cc(0), None, ALU.mult))
                            st.do(V.scalar_tensor_tensor(at, slot(j)[:, g2 * HD:(g2 + 1) * HD], cc(1), at, ALU.mult, ALU.add))
                            ins = V.scalar_tensor_tensor(at, slot(j)[:, 512 + g2 * HD:512 + (g2 + 1) * HD], cc(2), at, ALU.mult, ALU.add)
                            if g2 == 0:
                                st.do(ins)
                            else:
                                give(ins, j)
                st.end(HPG)
            with dve.Fori(0, DB // 2) as it:
                st.begin(it, 12)
                J = J_S
                take(dve, J + 1, it=it, per=S_PER)
                give(V.tensor_copy(ksT[1], slot(J + 1)), J + 1)
                take(dve, J + 3, it=it, per=S_PER)
                V.tensor_reduce(sv[:, 0:1], slot(J + 3)[:, 528:528 + NCS], AX.X, ALU.max, negate=True)
                V.tensor_copy(snew, slot(J + 3)[:, 512:528])
                V.tensor_reduce(sv[:, 1:2], slot(J + 3)[:, 0:WIN], AX.X, ALU.max, negate=True)
                st.do(V.tensor_reduce(sv[:, 2:3], slot(J + 3)[:, 520:528], AX.X, ALU.max, negate=True))
                V.tensor_tensor(sv[:, 3:4], sv[:, 1:2], sv[:, 2:3], ALU.min).then_inc(s_snew, 1)
                dve.wait_ge(s_expc, it + 1)
                st.do(V.reciprocal(sv[:, 20:21], sv[:, 24:25]))
                V.tensor_scalar(pcn[:, 0:NCS], Ps[:, CMP0:PW], sv[:, 20:21], None, ALU.mult).then_inc(s_pcn, 1)
                take(dve, J + 6, it=it, per=S_PER)
                give(V.tensor_copy(imp[:, 0, :], slot(J + 6)[:, 0:NSELB]), J + 6)
                take(dve, J + 7, it=it, per=S_PER)
                give(V.tensor_tensor(imp[:, 1, :], slot(J + 7)[:, 0:NSELB], bonus[:, :], ALU.add), J + 7)
                result_of(dve, J + 7, it=it, per=S_PER)
                st.do(V.tensor_reduce(sv[:, 7:8], imp[:, 1, :], AX.X, ALU.min))
                st.do(V.tensor_scalar(imp[:, 2, :], imp[:, 1, :], sv[:, 7:8], None, ALU.is_equal))
                st.do(V.tensor_tensor(imp[:, 3, :], imp[:, 2, :], jidx[:, :], ALU.mult))
                st.do(V.tensor_reduce(sv[:, 8:9], imp[:, 3, :], AX.X, ALU.max))
                st.do(V.tensor_scalar(imp[:, 4, :], jidx[:, :], sv[:, 8:9], NEG, ALU.is_equal, ALU.mult))
                take(dve, J + 4, it=it, per=S_PER)
                for hf in range(2):
                    sl = slot(J + 4)[:, hf * 512:(hf + 1) * 512].rearrange("p (r b n) -> p r b n", r=4, n=16)
                    dropped = imp[:, 4, hf * 8:(hf + 1) * 8].unsqueeze(1).unsqueeze(3).to_broadcast([P, 4, 8, 16])
                    ins = V.tensor_tensor(sl, sl, dropped, ALU.add)
                st.do(ins)
                V.tensor_reduce(sv[:, 4:5], slot(J + 4), AX.X, ALU.max, negate=True)
                st.do(V.tensor_reduce(sv[:, 5:6], snew[:, 0:DS], AX.X, ALU.max, negate=True))
                V.tensor_tensor(sv[:, 6:7], sv[:, 4:5], sv[:, 5:6], ALU.min).then_inc(s_maxs, 1)
                dve.wait_ge(s_exps, it + 1)
                V.tensor_tensor(sv[:, 25:26], sv[:, 9:10], sv[:, 10:11], ALU.add)
                st.do(V.tensor_tensor(sv[:, 26:27], sv[:, 11:12], sv[:, 12:13], ALU.add))
                st.do(V.reciprocal(sv[:, 28:31], sv[:, 24:27]))
                dve.wait_ge(s_gs, 16 * DB)
                st.do(V.tensor_tensor(sv[:, 32:35], sv[:, 28:31], gS[:, bass.ds(it, 1), :].rearrange("p a b -> p (a b)"), ALU.mult))
                for lo, hi, c in ((0, PAST, 1), (PAST, PAST + WIN, 2), (CMP0 - 2 * DS, CMP0 - DS, 1), (CMP0 - DS, CMP0, 2), (CMP0, PW, 0)):
                    V.tensor_scalar(Ps[:, lo:hi], Ps[:, lo:hi], sv[:, 32 + c:33 + c], None, ALU.mult).then_inc(s_scaled, 1)
                take(dve, J + 8, it=it, per=S_PER)
                give(V.tensor_copy(PTs[:, 0:8, :].rearrange("p a b -> p (a b)"), slot(J + 8)), J + 8)
                take(dve, J + 10, it=it, per=S_PER)
                for g in range(NKV):
                    r = slice(g * HD, (g + 1) * HD)
                    last = V.tensor_copy(oT[r, :, bass.ds(it * (2 * DS) + SEQ, DS)], slot(J + 10)[r, g * 32:(g + 1) * 32].rearrange("p (c t) -> p c t", t=DS))
                give(last, J + 10)
                st.end(DB // 2)
            take(dve, J_LN)
            for c in range(CC):
                ins = V.tensor_tensor(cv[:, c, :], cv[:, c, :], slot(J_LN)[:, 0:T], ALU.subtract)
                if c < CC - 1:
                    ins.then_inc(s_xc, 1)
                else:
                    give(ins, J_LN)
            result_of(dve, J_LN)
            take(dve, J_LN + 1)
            give(V.tensor_scalar(rstd, slot(J_LN + 1)[:, 0:T], EPS, None, ALU.add), J_LN + 1)
            dve.wait_ge(s_var, 1)
            st.do(V.reciprocal(rstd, rstd))
            for c in range(CC):
                V.tensor_tensor(cv[:, c, :], cv[:, c, :], rstd, ALU.mult).then_inc(s_cn, 1)
            for m in range(KD):
                j = J_OUT + 2 * m
                take(dve, j)
                if m:
                    dve.wait_ge(s_merged, m)
                give(V.tensor_tensor(mt[:, 0, :], slot(j)[:, 0:T], mgT[:, m, :], ALU.mult), j)
                take(dve, j + 1)
                give(V.tensor_tensor(mt[:, 1, :], slot(j + 1)[:, 0:T], mgT[:, KD + m, :], ALU.mult), j + 1)
                result_of(dve, j)
                result_of(dve, j + 1)
                V.tensor_tensor(xT[:, m, :], mt[:, 0, :], mt[:, 1, :], ALU.add).then_inc(s_merged, 1)
            for i in range(NT):
                take(dve, J_WO + i)
                r = on(h, i)
                give(V.tensor_tensor(h[r, i, :], h[r, i, :], slot(J_WO + i)[r, :], ALU.add), J_WO + i)
            dve.wait_ge(s_pow, 2)
            for i in range(NT):
                r = on(h, i)
                V.tensor_scalar(xs2[r, i, :], h[r, i, :], rs[r, 1, i:i + 1], None, ALU.mult).then_inc(s_xs, 1)
            for k in range(0, KD, 2):
                take(dve, J_N2 + k)
                give(V.tensor_scalar(xT[:, k, :], slot(J_N2 + k)[:, 0:T], gffn[:, k:k + 1], None, ALU.mult), J_N2 + k)
            st.do(V.memset(lg, 0.0))
            dve.wait_ge(s_wr, 16 * 6)
            take(dve, J_RT)
            for i in range(NT):
                r = on(h, i)
                last = V.tensor_tensor(lg[r, i, :], slot(J_RT)[r, i * NR:(i + 1) * NR], brow[r, :], ALU.add)
            give(last, J_RT)
            result_of(dve, J_RT)
            lgG, lgE = lg[:, :, 0:NG], lg[:, :, NG:NR].rearrange("p t (g e) -> p t g e", g=NG)
            v3 = lambda n, w: rt[:, n, 0:NT * w].rearrange("p (t w) -> p t w", w=w)
            wide = lambda x, w: x.to_broadcast([P, NT, w])

            def first_best(best, eq, x, w, idx, out):
                st.do(V.tensor_reduce(best[:, :, 0], x, AX.X, ALU.max))
                st.do(V.tensor_tensor(eq, x, wide(best, w), ALU.is_equal))
                ib = idx.unsqueeze(1).to_broadcast([P, NT, w])
                st.do(V.tensor_tensor(eq, eq, ib, ALU.mult))
                st.do(V.tensor_reduce(v3(19, 1)[:, :, 0], eq, AX.X, ALU.max))
                st.do(V.tensor_tensor(out, ib, wide(v3(19, 1), w), ALU.is_equal))

            gm, gsel, leg, oh1, oh2 = v3(0, 1), v3(2, NG), v3(7, EPG), v3(9, EPG), v3(11, EPG)
            first_best(gm, v3(1, NG), lgG, NG, cidx[:, 0:NG], gsel)
            V.tensor_tensor(v3(5, NG), lgG, wide(gm, NG), ALU.subtract).then_inc(s_sub, 1)
            pick = rt[:, 6, 0:NT * NE].rearrange("p (t g e) -> p t g e", g=NG, e=EPG)
            st.do(V.tensor_tensor(pick, lgE, gsel.unsqueeze(3).to_broadcast([P, NT, NG, EPG]), ALU.mult))
            st.do(V.tensor_reduce(leg, pick.rearrange("p t g e -> p t e g"), AX.X, ALU.add))
            first_best(v3(3, 1), v3(8, EPG), leg, EPG, cidx[:, NG:NG + EPG], oh1)
            st.do(V.scalar_tensor_tensor(v3(10, EPG), oh1, NEG, leg, ALU.mult, ALU.add))
            first_best(v3(4, 1), v3(8, EPG), v3(10, EPG), EPG, cidx[:, NG:NG + EPG], oh2)
            V.tensor_tensor(rt[:, 12, 0:NT], rt[:, 4, 0:NT], rt[:, 3, 0:NT], ALU.subtract).then_inc(s_sub, 1)
            dve.wait_ge(s_ex, 2)
            st.do(V.tensor_reduce(rt[:, 13, 0:NT], v3(5, NG), AX.X, ALU.add))
            V.tensor_scalar(rt[:, 14, 0:NT], rt[:, 12, 0:NT], 1.0, None, ALU.add)
            st.do(V.reciprocal(rt[:, 13, 0:NT], rt[:, 13, 0:NT]))
            st.do(V.reciprocal(rt[:, 14, 0:NT], rt[:, 14, 0:NT]))
            st.do(V.tensor_tensor(rt[:, 15, 0:NT], rt[:, 13, 0:NT], rt[:, 14, 0:NT], ALU.mult))
            st.do(V.tensor_tensor(rt[:, 16, 0:NT], rt[:, 15, 0:NT], rt[:, 12, 0:NT], ALU.mult))
            by_e = lambda x: x.rearrange("p t (g e) -> p t g e", g=NG)
            first, second, either = v3(20, NE), v3(21, NE), v3(22, NE)
            for oh, out in ((oh1, first), (oh2, second)):
                st.do(V.tensor_tensor(by_e(out), gsel.unsqueeze(3).to_broadcast([P, NT, NG, EPG]),
                                      oh.unsqueeze(2).to_broadcast([P, NT, NG, EPG]), ALU.mult))
            V.tensor_tensor(either, first, second, ALU.add).then_inc(s_sub, 1)
            st.do(V.memset(run[0], 0.0))
            st.do(V.memset(run[1], 0.0))
            take(dve, J_POS)
            give(V.tensor_scalar(place, slot(J_POS)[:, 0:2 * NT * NE], float(C), None, ALU.mult), J_POS)
            result_of(dve, J_POS)
            c0 = NG + EPG
            e_row, blocks, limits = cidx[:, c0:c0 + NE], cidx[:, c0 + NE:c0 + NE + N_OVER], cidx[:, c0 + NE + N_OVER:N_CIDX]
            before = place[:, 0:NT * NE]
            tile_ends = place[:, NT * NE:2 * NT * NE]
            for i in range(1, NT):
                n = slice(i * NE, (i + 1) * NE)
                st.do(V.tensor_tensor(tile_ends[:, n], tile_ends[:, n], tile_ends[:, (i - 1) * NE:i * NE], ALU.add))
            total = tile_ends[:, (NT - 1) * NE:]
            st.do(V.tensor_tensor(before[:, NE:], before[:, NE:], tile_ends[:, 0:(NT - 1) * NE], ALU.add))
            cells = lambda n, w: grid[:, 0:n * w].rearrange("p (n w) -> p n w", w=w)
            over = cells(NE, MAX_OVER)
            st.do(V.tensor_tensor(over, total.unsqueeze(2).to_broadcast([P, NE, MAX_OVER]), limits.unsqueeze(1).to_broadcast([P, NE, MAX_OVER]), ALU.is_gt))
            n_over = rt[:, 23, 0:NE]
            st.do(V.tensor_reduce(n_over, over, AX.X, ALU.add))
            st.do(V.tensor_copy(run[0][:, 16:16 + NE], n_over))
            src = 0
            for step in (1, 2, 4, 8, 16):
                st.do(V.tensor_tensor(run[1 - src][:, 16:16 + NE], run[src][:, 16:16 + NE], run[src][:, 16 - step:16 - step + NE], ALU.add))
                src = 1 - src
            ends = run[src][:, 16:16 + NE]
            shift = rt[:, 25, 0:NE]
            st.do(V.tensor_tensor(shift, ends, n_over, ALU.subtract))
            st.do(V.tensor_scalar(shift, shift, float(BR), float(BR * (NE - 1)), ALU.mult, ALU.add))
            st.do(V.tensor_tensor(shift, shift, e_row, ALU.subtract))
            both = rt[:, 20:22, 0:NT * NE].rearrange("p c x -> p (c x)")
            prod = rt[:, 0:2, 0:NT * NE].rearrange("p c x -> p (c x)")
            prod_t = prod.rearrange("p (t e) -> p t e", e=NE)
            at, row, jump = rt[:, 6, 0:2 * NT], rt[:, 7, 0:2 * NT], rt[:, 8, 0:2 * NT]
            st.do(V.tensor_tensor(prod.rearrange("p (c x) -> p c x", c=2), both.rearrange("p (c x) -> p c x", c=2),
                                  before.unsqueeze(1).to_broadcast([P, 2, NT * NE]), ALU.mult))
            st.do(V.tensor_reduce(at, prod_t, AX.X, ALU.add))
            for out, by_expert in ((row, e_row), (jump, shift)):
                st.do(V.tensor_tensor(prod_t, both.rearrange("p (t e) -> p t e", e=NE), by_expert.unsqueeze(1).to_broadcast([P, 2 * NT, NE]), ALU.mult))
                st.do(V.tensor_reduce(out, prod_t, AX.X, ALU.add))
            st.do(V.tensor_tensor(row, row, at, ALU.add))
            st.do(V.scalar_tensor_tensor(jump, at, float(BR), jump, ALU.is_ge, ALU.mult))
            V.tensor_tensor(dest[:, :, :].rearrange("p a b -> p b a"), row.rearrange("p (b a) -> p b a", b=2),
                            jump.rearrange("p (b a) -> p b a", b=2), ALU.add).then_inc(s_dest, 1)
            owner = cells(N_OVER, NE)
            st.do(V.tensor_tensor(owner, ends.unsqueeze(1).to_broadcast([P, N_OVER, NE]), blocks.unsqueeze(2).to_broadcast([P, N_OVER, NE]), ALU.is_le))
            owners = rt[:, 24, 0:N_OVER]
            st.do(V.tensor_reduce(owners, owner, AX.X, ALU.add))
            V.tensor_copy(eid[:, 0:N_OVER], owners).then_inc(s_eid, 1)
            V.tensor_scalar(eid[:, N_OVER:], owners, float(NE - 1), None, ALU.min).then_inc(s_eid, 1)
            def put_rows(j, s, it=None, used=True):
                take(dve, *([j, j - 7] if used else [j]), it=it, per=E_PER)
                g = gffn2[:, :].unsqueeze(2).to_broadcast([P, KD, P])
                give(V.tensor_tensor(xeT[s], slot(j).rearrange("p (k c) -> p k c", c=P), g, ALU.mult), j)

            def gate_up(j, s, n_sil, it=None, used=True):
                take(dve, *([j + 1, j - 5] if used else [j + 1]), it=it, per=E_PER)
                dve.wait_ge(s_sil, n_sil)
                give(V.tensor_tensor(hid[s], slot(j + 1)[:, 512:512 + P], sil[s], ALU.mult), j + 1)

            for p in range(2):
                put_rows(J_MOE + 4 * p, p, used=False)
            for p in range(2):
                gate_up(J_MOE + 4 * p, p, p + 1, used=False)
                put_rows(J_MOE + 4 * (p + 2), p)
            loops = (NUSUAL - 4) // 2
            with dve.Fori(0, loops) as it:
                for u in range(2):
                    gate_up(J_MOE + 4 * (u + 2), u, it * 2 + (u + 3), it)
                    put_rows(J_MOE + 4 * (u + 4), u, it)
            for p in range(2 + 2 * loops, NUSUAL):
                gate_up(J_MOE + 4 * p, p % 2, p + 1)
                if p + 2 < NUSUAL:
                    put_rows(J_MOE + 4 * (p + 2), p % 2)
            dve.wait_ge(s_eid, 2)
            more = more_blocks(dve)
            with dve.If(more < NE):
                for p in (NUSUAL, NUSUAL + 1):
                    put_rows(J_MOE + 4 * p, p % 2)
                for p in range(NUSUAL, NPAIR):
                    gate_up(J_MOE + 4 * p, p % 2, p + 1)
                    if p + 2 < NPAIR:
                        put_rows(J_MOE + 4 * (p + 2), p % 2)
            for i in range(NT):
                r = on(h, i)
                dve.wait_ge(s_got[i], 32)
                st.do(V.scalar_tensor_tensor(h[r, i, :], got[0][r, i, :], rt[r, 15, i:i + 1], h[r, i, :], ALU.mult, ALU.add))
                V.scalar_tensor_tensor(h[r, i, :], got[1][r, i, :], rt[r, 16, i:i + 1], h[r, i, :], ALU.mult, ALU.add).then_inc(s_hy, 1)
            dve.wait_ge(s_pow, 3)
            dve.wait_ge(s_gfin, 16)
            for i in range(NT):
                r = on(h, i)
                V.scalar_tensor_tensor(h[r, i, :], h[r, i, :], rs[r, 2, i:i + 1], gfin[r, :], ALU.mult, ALU.mult).then_inc(s_final, 1)

        @block.tensor
        def _(pe):
            mm = nc.tensor.matmul
            tr = nc.tensor.transpose

            def norm_transposes(j0, src):
                for k in range(KD):
                    claim(pe, j0 + k)
                    for i in range(NT):
                        n = TS[i]
                        last = tr(slot(j0 + k)[:, i * P:i * P + n], src[0:n, i, k * P:(k + 1) * P], ident[0:n, 0:n])
                    fill(last, j0 + k)

            def project(j, weights, x, n_k, it=None, per=0):
                claim(pe, j, it, per)
                for lo, hi in ((0, 512), (512, T)):
                    for k in range(n_k):
                        last = mm(slot(j)[:, lo:hi], weights(k), x[:, k, lo:hi], start=k == 0, stop=k == n_k - 1)
                fill(last, j)

            pe.wait_ge(s_first, 16 * len(firsts))
            pe.wait_ge(s_xs, NT)
            norm_transposes(J_NORM, xs)
            for k in range(KD - 4, KD):
                result_of(pe, J_NORM + k)
            pe.wait_ge(s_wkv, 16)
            for i in range(NT):
                j = J_KV + i
                claim(pe, j)
                for lo, hi in ((0, 512), (512, KVN)):
                    for k in range(KD):
                        last = mm(slot(j)[on(h, i), lo:hi], xT[:, k, i * P:i * P + TS[i]], wkv[:, k, lo:hi], start=k == 0, stop=k == KD - 1)
                fill(last, j)
            for n in range(2 * CC):
                pe.wait_ge(s_wring[n % 4], 16 * (n // 4 + 1))
                project(J_GLU + n, lambda k: wring[n % 4][:, k, :], xT, KD)
            pe.wait_ge(s_rope, NT)
            for s in range(2):
                claim(pe, J_KT + s)
                for i in range(NT):
                    last = tr(slot(J_KT + s)[:, i * P:i * P + TS[i]], rot[on(h, i), i, s, :], ident[on(h, i), on(h, i)])
                fill(last, J_KT + s)
            pe.wait_ge(s_cst, 32)
            claim(pe, J_CST)
            for c in range(CC):
                for half in range(2):
                    at = (c // 2) * 512 + (c % 2) * 240 + half * 120
                    last = tr(slot(J_CST)[:, at:at + 120], cst[0:120, half, c * P:(c + 1) * P], ident[0:120, 0:120])
            fill(last, J_CST)
            claim(pe, J_WDW)
            for c in range(CC):
                last = tr(slot(J_WDW)[:, c * TAPS:(c + 1) * TAPS], wdr[:, c * P:(c + 1) * P], ident[0:TAPS, 0:TAPS])
            fill(last, J_WDW)
            claim(pe, J_CSO)
            for c in range(CC):
                result_of(pe, J_GLU + 2 * c + 1)
            for c in range(CC):
                tr(slot(J_CSO)[0:PAD, c * P:(c + 1) * P], aP[:, c, SEQ:SEQ + PAD], ident[:, :])
                last = tr(slot(J_CSO)[0:NS_TOK, C + c * P:C + (c + 1) * P], anew[:, c, :], ident[:, :])
            fill(last, J_CSO)
            pe.wait_ge(s_const, ALL_CONST)
            with pe.Fori(0, 4) as it:
                for u in range(4):
                    pe.wait_ge(s_wring[u], it * 16 + 48)
                    project(J_MG + u, lambda k: wring[u][:, k, :], xT, KD, it, 4)
            for s, j0 in enumerate((J_CMP, J_CMPV)):
                with pe.Fori(0, 2) as it:
                    for u in range(4):
                        n = u // 2
                        if u % 2 == 0:
                            pe.wait_ge(s_raw[n], it * 16 + (16 + (48 if n == 0 else 32) * s))
                        claim(pe, j0 + u, it, 4)
                        for k in range(KD):
                            last = tr(slot(j0 + u)[:, k * P:(k + 1) * P], raw[n][:, (u % 2) * KD + k, :], ident[:, :])
                        fill(last, j0 + u)
                pe.wait_ge(s_raw[0], 48 * (s + 1))
                claim(pe, j0 + DB)
                for k in range(16):
                    last = tr(slot(j0 + DB)[:, k * STR_P:(k + 1) * STR_P], raw[0][0:STR_P, k, :], ident[0:STR_P, 0:STR_P])
                fill(last, j0 + DB)
                pe.wait_ge(s_w1, 32 * (s + 1))
                for u in range(5, DB + 1):
                    result_of(pe, j0 + u)
                claim(pe, j0 + DB + 1)
                for g in range(NKV):
                    for k in range(KD):
                        last = mm(slot(j0 + DB + 1)[:, g * 512:(g + 1) * 512], w1[:, k, :], XT[:, g, k, 0:STR_S], start=k == 0, stop=k == KD - 1)
                fill(last, j0 + DB + 1)
                claim(pe, j0 + DB + 2)
                for g in range(NKV):
                    for k in range(KD):
                        last = mm(slot(j0 + DB + 2)[:, g * STR_P:(g + 1) * STR_P], w1[:, k, :], XT[:, g, k, STR_S:STR], start=k == 0, stop=k == KD - 1)
                fill(last, j0 + DB + 2)
                pe.wait_ge(s_silu, s + 1)
                claim(pe, j0 + DB + 3)
                if s == 0:
                    for g in range(NKV):
                        r = slice(g * HD, (g + 1) * HD)
                        mm(slot(j0 + DB + 3)[r, 0:512], w2[:, 0, :], upper[:, g, 0:512], start=True, stop=True)
                        last = mm(slot(j0 + DB + 3)[r, 512:STR], w2[:, 0, :], upper[:, g, 512:STR], start=True, stop=True)
                    fill(last, j0 + DB + 3)
                else:
                    for b in range(DB):
                        for g in range(NKV):
                            last = mm(slot(j0 + DB + 3)[0:HD, b * P + g * HD:b * P + (g + 1) * HD], upper[:, g, b * HD:(b + 1) * HD], w2[:, 1, :], start=True, stop=True)
                    fill(last, j0 + DB + 3)
                    claim(pe, j0 + DB + 4)
                    for g in range(NKV):
                        last = mm(slot(j0 + DB + 4)[0:32, g * HD:(g + 1) * HD], upper[:, g, STR_S:STR], w2[:, 1, :], start=True, stop=True)
                    fill(last, j0 + DB + 4)
            for j in (J_CMP + DB + 3, J_CMPV + DB + 3, J_CMPV + DB + 4):
                result_of(pe, j)
            pe.wait_ge(s_anyok, 1)
            with pe.Fori(0, 2) as it2:
                for u2 in range(2):
                    W = 2 * Q_PER
                    off = u2 * Q_PER
                    pe.wait_ge(s_wq[u2], it2 * 32 + 32)
                    project(J_Q + off, lambda k: wq[u2][:, k, :], xT, KD, it2, W)
                    result_of(pe, J_Q + off, it=it2, per=W)
                    claim(pe, J_Q + 1 + off, it2, W)
                    mm(slot(J_Q + 1)[:, 0:512], perm[:, :], qT[:, 0:512], start=True, stop=True)
                    fill(mm(slot(J_Q + 1)[:, 512:T], perm[:, :], qT[:, 512:T], start=True, stop=True), J_Q + 1)
                    pe.wait_ge(s_qrot, it2 * 2 + (u2 + 1))
                    for kind, qt, g in order:
                        j = job_of[(kind, qt, g)]
                        nb = qt + 1
                        hd = slice(g * HD, (g + 1) * HD)
                        qc = slice(qt * P, (qt + 1) * P)
                        if kind == "S":
                            claim(pe, j + off, it2, W)
                            for br in range(2):
                                mm(slot(j)[:, br * 512:br * 512 + nb * P], qrot[hd, qc], kT[hd, br, 0:nb * P], start=True, stop=False, skip_group_check=True)
                                last = mm(slot(j)[:, br * 512 + qt * P:br * 512 + nb * P], identb[:, :], causal[:, :], start=False, stop=True, skip_group_check=True)
                            fill(last, j)
                        if kind == "C":
                            claim(pe, j + off, it2, W)
                            for g2 in range(NKV):
                                h2 = slice(g2 * HD, (g2 + 1) * HD)
                                mm(slot(j)[:, g2 * 512:g2 * 512 + NCP], qT[h2, qc], kcT[h2, STR_S:STR_S + NCP], start=True, stop=False, skip_group_check=True)
                                last = mm(slot(j)[:, g2 * 512:g2 * 512 + NCP], identb[:, :], cmask[:, qt, 0:NCP], start=False, stop=True, skip_group_check=True)
                            fill(last, j)
                        if kind == "T":
                            claim(pe, j + off, it2, W, after=[job_of[("S", qt, g)] + off])
                            for br in range(2):
                                for b in range(nb):
                                    last = tr(slot(j)[:, br * 512 + b * P:br * 512 + (b + 1) * P], Pb[(2 * qt + g) % 4][:, br, b * P:(b + 1) * P], ident[:, :])
                            fill(last, j)
                        if kind == "TC":
                            claim(pe, j + off, it2, W, after=[job_of[("C", qt, 0)] + off])
                            for g2 in range(NKV):
                                last = tr(slot(j)[0:NCP, g2 * P:(g2 + 1) * P], Pc[qt % 2][:, g2, 0:NCP], ident[:, :])
                            fill(last, j)
                        if kind == "O":
                            claim(pe, j + off, it2, W, after=[job_of[x] + off for x in (("T", qt, 0), ("T", qt, 1), ("TC", qt, 0))])
                            for g2 in range(NKV):
                                h2 = slice(g2 * HD, (g2 + 1) * HD)
                                for br, vat in ((0, 3 * P), (1, 5 * P)):
                                    for b in range(nb):
                                        mm(slot(j)[:, br * 512 + g2 * HD:br * 512 + (g2 + 1) * HD], PT[g2][:, br, b * P:(b + 1) * P],
                                           kv[:, b, vat + g2 * HD:vat + (g2 + 1) * HD], start=b == 0, stop=b == nb - 1)
                                last = mm(slot(j)[:, 128 + g2 * HD:128 + (g2 + 1) * HD], PcT[0:NCP, g2, :], vcP[0:NCP, h2], start=True, stop=True)
                            fill(last, j)
                        if kind == "OT":
                            claim(pe, j + off, it2, W, after=[job_of[("O", 2 * qt + n, 0)] + off for n in range(2)])
                            for n in range(2):
                                last = tr(slot(j)[:, n * P:(n + 1) * P], otok[:, 2 * qt + n, :], ident[:, :])
                            fill(last, j)
            with pe.Fori(0, DB // 2) as it:
                J = J_S
                for b in range(2):
                    pe.wait_ge(s_kin[b], it * 32 + 32)
                    claim(pe, J + b, it, S_PER)
                    for p in range(NPG):
                        last = tr(slot(J + b)[:, p * P:(p + 1) * P], kraw[b][:, p, :], ident[:, :])
                    fill(last, J + b)
                pe.wait_ge(s_kw, it * 32 + 32)
                claim(pe, J + 2, it, S_PER)
                for b in range(2):
                    for w in range(WB):
                        last = tr(slot(J + 2)[:, b * 512 + w * P:b * 512 + (w + 1) * P], kwraw[:, b, w, :], ident[:, :])
                fill(last, J + 2)
                result_of(pe, J + 2, it=it, per=S_PER)
                pe.wait_ge(s_qbd, it + 1)
                claim(pe, J + 3, it, S_PER)
                S = slot(J + 3)
                for b in range(2):
                    mm(S[b * 64:b * 64 + 64, 0:WIN], qbd[:, 1, b, :], kwT[:, b, :], start=True, stop=False, skip_group_check=True)
                mm(S[:, 0:DS], identb[:, :], rmask[:, 0, :], start=False, stop=True, skip_group_check=True)
                for b in range(2):
                    mm(S[b * 64:b * 64 + 64, 512:528], qbd[:, 1, b, :], kdyn[:, b, 0:2 * DS], start=True, stop=False, skip_group_check=True)
                for n in range(2):
                    mm(S[:, 512 + n * DS:512 + (n + 1) * DS], identb[:, :], rmask[:, 1, :], start=False, stop=True, skip_group_check=True)
                for b in range(2):
                    last = mm(S[b * 64:b * 64 + 64, 528:528 + NCS], qbd[:, 0, b, :], kdyn[:, b, 2 * DS:2 * DS + NCS], start=True, stop=True, skip_group_check=True)
                fill(last, J + 3)
                claim(pe, J + 4, it, S_PER, after=(J, J + 1))
                for b in range(2):
                    for n in range(2):
                        last = mm(slot(J + 4)[b * 64:b * 64 + 64, n * 512:(n + 1) * 512], qbd[:, 1, b, :], ksT[b][:, n * 512:(n + 1) * 512], start=True, stop=True)
                fill(last, J + 4)
                pe.wait_ge(s_pcn, it + 1)
                claim(pe, J + 5, it, S_PER)
                fill(tr(slot(J + 5)[:, 0:P], pcn, ident[:, :]), J + 5)
                result_of(pe, J + 5, it=it, per=S_PER)
                claim(pe, J + 6, it, S_PER)
                fill(mm(slot(J + 6)[:, 0:NSELB], PTn[0:NCS, 2, :], ovl[0:NCS, :], start=True, stop=True), J + 6)
                result_of(pe, J + 6, it=it, per=S_PER)
                claim(pe, J + 7, it, S_PER)
                fill(mm(slot(J + 7)[:, 0:NSELB], hsum[:, :], imp[:, 0, :], start=True, stop=True), J + 7)
                pe.wait_ge(s_scaled, it * 5 + 5)
                claim(pe, J + 8, it, S_PER)
                for n in range(8):
                    last = tr(slot(J + 8)[:, n * P:(n + 1) * P], Ps[:, n * P:(n + 1) * P], ident[:, :])
                fill(last, J + 8)
                claim(pe, J + 9, it, S_PER)
                for n in range(4):
                    tr(slot(J + 9)[:, n * P:(n + 1) * P], Ps[:, (8 + n) * P:(9 + n) * P], ident[:, :])
                for n in range(2):
                    tr(slot(J + 9)[0:DS, 512 + n * P:512 + (n + 1) * P], Ps[:, CMP0 - 2 * DS + n * DS:CMP0 - DS + n * DS], ident[:, :])
                fill(tr(slot(J + 9)[0:NCS, 768:896], Ps[:, CMP0:PW], ident[:, :]), J + 9)
                result_of(pe, J + 8, J + 9, it=it, per=S_PER)
                pe.wait_ge(s_vw, it * 96 + 96)
                pe.wait_ge(s_vst, it + 1)
                for b in range(2):
                    pe.wait_ge(s_vin[b], it * 32 + 32)
                    claim(pe, J + 10 + b, it, S_PER)
                    cols = slice(b * 64, b * 64 + 64)
                    O = slot(J + 10 + b)[:, 0:64]
                    for n in range(8):
                        mm(O, vsel[b][:, n, :], PTs[:, n, cols], start=n == 0, stop=False)
                    for n in range(WB):
                        mm(O, vwin[:, b, n, :], PTs[:, 8 + n, cols], start=False, stop=False)
                    for n in range(2):
                        mm(O, vst[0:DS, b, n, :], PTn[0:DS, n, cols], start=False, stop=False)
                    fill(mm(O, vst[0:NCS, b, 2, :], PTn[0:NCS, 2, cols], start=False, stop=True), J + 10 + b)
            pe.wait_ge(s_conv, 2 * CC * TAPS)
            claim(pe, J_LN)
            for lo, hi in ((0, 512), (512, T)):
                for c in range(CC):
                    last = mm(slot(J_LN)[:, lo:hi], onesC[:, :], cv[:, c, lo:hi], start=c == 0, stop=c == CC - 1)
            fill(last, J_LN)
            pe.wait_ge(s_sqd, CC)
            claim(pe, J_LN + 1)
            for lo, hi in ((0, 512), (512, T)):
                for c in range(CC):
                    last = mm(slot(J_LN + 1)[:, lo:hi], onesC[:, :], sq[:, c, lo:hi], start=c == 0, stop=c == CC - 1)
            fill(last, J_LN + 1)
            pe.wait_ge(s_silc, CC)
            pe.wait_ge(s_wout, 16 * (1 + 2 * HPG))
            result_of(pe, J_S + S_PER * (DB // 2) - 2)
            result_of(pe, J_S + S_PER * (DB // 2) - 1)
            result_of(pe, J_Q + Q_PER * HPG - 1)
            for m in range(KD):
                mc = slice(m * P, (m + 1) * P)
                project(J_OUT + 2 * m, lambda k: wco[:, k, mc], cv, CC)
                project(J_OUT + 2 * m + 1, lambda k: wno[k][:, mc], oT, HPG)
            pe.wait_ge(s_wo, 16)
            pe.wait_ge(s_merged, KD)
            for i in range(NT):
                j = J_WO + i
                claim(pe, j)
                for lo in (0, 512):
                    for k in range(KD):
                        last = mm(slot(j)[on(h, i), lo:lo + 512], xT[:, k, i * P:i * P + TS[i]], wo[:, k, lo:lo + 512], start=k == 0, stop=k == KD - 1)
                fill(last, j)
            pe.wait_ge(s_xs, 2 * NT)
            norm_transposes(J_N2, xs2)
            for k in range(KD - 4, KD):
                result_of(pe, J_N2 + k)
            pe.wait_ge(s_wr, 16 * 6)
            claim(pe, J_RT)
            for i in range(NT):
                for k in range(KD):
                    last = mm(slot(J_RT)[on(h, i), i * NR:(i + 1) * NR], xT[:, k, i * P:i * P + TS[i]], wr[:, k, :], start=k == 0, stop=k == KD - 1)
            fill(last, J_RT)
            pe.wait_ge(s_sub, 3)
            claim(pe, J_POS)
            for weights, at in ((tri, 0), (onesC[:, :], NT * NE)):
                for r, lo, hi in ((slice(0, P), 0, QT * NE), (on(h, QT), QT * NE, NT * NE)):
                    last = mm(slot(J_POS)[:, at + lo:at + hi], weights[r, :], rt[r, 22, lo:hi], start=True, stop=True)
            fill(last, J_POS)

            def turn(j, s, n_x, it=None):
                pe.wait_ge(s_xe[s], n_x)
                claim(pe, j, it, 2 * E_PER)
                for k in range(KD):
                    last = tr(slot(j)[:, k * P:(k + 1) * P], xe[s].rearrange("c (p k) -> c p k", k=KD)[:, :, k], ident[:, :])
                fill(last, j)

            def gates_ups(j, s, n_w, it=None):
                claim(pe, j + 1, it, 2 * E_PER, after=(j,))
                pe.wait_ge(s_we[s], n_w)
                for u in range(2):
                    for w, at in ((wgate, 0), (wup, 512)):
                        for k in range(KD):
                            last = mm(slot(j + 1)[:, at + u * BR:at + (u + 1) * BR], w[s][:, u, k, :], xeT[s][:, k, u * BR:(u + 1) * BR],
                                      start=k == 0, stop=k == KD - 1)
                fill(last, j + 1)

            def downs(j, s, n_w, it=None):
                for half in range(2):
                    claim(pe, j + 2 + half, it, 2 * E_PER, after=(j + 1,) if half == 0 else ())
                    if half == 0:
                        pe.wait_ge(s_wd[s], n_w)
                    for u in range(2):
                        last = mm(slot(j + 2 + half)[u * BR:(u + 1) * BR, 0:512], hid[s][:, u * BR:(u + 1) * BR],
                                  wdn[s][:, u, half * 512:(half + 1) * 512], start=True, stop=True)
                    fill(last, j + 2 + half)

            def step(p, j, it, n_x, n_w, n_d):
                gates_ups(j, p % 2, n_w, it)
                if n_x is not None:
                    turn(j + 8, (p + 2) % 4, n_x, it)
                downs(j, p % 2, n_d, it)

            def steps(p0, p1):
                for p in range(p0, p1):
                    step(p, J_MOE + 4 * p, None, 16 * ((p + 2) // 4 + 1) if p + 2 < p1 else None, loads(p, 2), loads(p, 1))

            for p in range(2):
                turn(J_MOE + 4 * p, p, 16)
            loops = NE // 8
            with pe.Fori(0, loops) as it:
                for u in range(4):
                    step(u, J_MOE + 4 * u, it, it * 16 + 16 * ((u + 2) // 4 + 1), it * 64 + 32 * (u // 2 + 1), it * 32 + 16 * (u // 2 + 1))
            steps(4 * loops, NUSUAL)
            pe.wait_ge(s_eid, 2)
            more = more_blocks(pe)
            with pe.If(more < NE):
                for p in (NUSUAL, NUSUAL + 1):
                    turn(J_MOE + 4 * p, p % 4, 16 * (p // 4 + 1))
                steps(NUSUAL, NPAIR)


WEIGHTS = ("x_prompt x_sample cache_k_cmp cache_v_cmp cache_k_sel cache_v_sel state_k_win state_v_win state_conv page_table g_mix "
           "w_in w_dw b_dw conv_norm_g conv_norm_b w_conv_out w_ck1 b_ck1 w_ck2 w_cv1 b_cv1 w_cv2 w_nsa_out w_o g_ffn w_rg b_rg "
           "w_re b_re w_gate w_up w_down g_final").split()
KVP, KVS = (1, 1, SEQ, NKV, HD), (1, DB, DS, NKV, HD)
OUTS = [("y_prompt", (1, SEQ, D)), ("y_sample", (DB, DS, D)),
        ("k_cmp_p", KVP), ("v_cmp_p", KVP), ("k_sel_p", KVP), ("v_sel_p", KVP), ("k_win_p", KVP), ("v_win_p", KVP), ("conv_p", (1, 1, PAD, C)),
        ("k_cmp_s", KVS), ("v_cmp_s", KVS), ("k_sel_s", KVS), ("v_sel_s", KVS),
        ("k_win_s", (1, DB, WIN, NKV, HD)), ("v_win_s", (1, DB, WIN, NKV, HD)), ("conv_s", (1, DB, PAD, C))]


def constants():
    f = np.float32

    def bf16(x):
        return (np.ascontiguousarray(x, f).view(np.uint32) >> 16).astype(np.uint16)

    pos = np.concatenate([np.arange(SEQ), np.tile(PAST + np.arange(DS), DB)]).astype(f)
    inv = (f(10000.0) ** (-np.arange(HD // 2, dtype=f) * f(2.0) / f(HD))).astype(f)
    ang = (pos[:, None] * inv[None, :]).astype(f)
    cos, sin = np.cos(ang).astype(f), np.sin(ang).astype(f)

    def by_row(x):
        full = np.zeros((NT * P, 32), f)
        full[:T] = x
        return np.ascontiguousarray(full.reshape(NT, P, 32).transpose(1, 0, 2))

    q = np.arange(P)
    t = np.arange(SEQ)
    n = np.arange(32)
    cmask = np.where(n[None, :] * 16 + 31 <= t[:, None], 0.0, NEG).reshape(QT, P, 32).transpose(1, 0, 2)
    row_t = q % DS
    j8 = np.arange(DS)
    rmask = np.stack([np.where(j8[None, :] <= row_t[:, None], NEG, 0.0), np.where(j8[None, :] <= row_t[:, None], 0.0, NEG)], 1)
    perm = np.zeros((P, P), f)
    for b in range(P):
        e = b % HD
        if e < 32:
            perm[b + 32, b] = -1.0
        else:
            perm[b - 32, b] = 1.0
    seq, g, tt = q // 64, q % 64 // 32, q % DS
    hs = ((seq[:, None] == seq) & (g[:, None] == g) & (tt[:, None] == tt)).astype(f)
    i, j = np.arange(HD)[:, None], np.arange(NSELB)[None, :]
    ov = ((i * 16 < (j + 1) * SELB) & (i * 16 + 32 > j * SELB)).astype(f)
    bonus = np.zeros((P, NSELB), f)
    bonus[:, [0, NSELB - 2, NSELB - 1]] = 1000.0
    return {
        "c_ident": np.eye(P, dtype=f), "c_identb": bf16(np.eye(P)),
        "c_causal": bf16(np.where(q[None, :] <= q[:, None], 0.0, NEG)), "c_cmask": bf16(cmask),
        "c_rmask": bf16(rmask), "c_perm": perm, "c_hsum": hs, "c_ovl": ov,
        "c_jidx": np.tile(np.arange(1, NSELB + 1, dtype=f), (P, 1)), "c_bonus": bonus,
        "c_anyok": (q >= 31).astype(f)[:, None], "c_ones": np.full((P, P), 1.0 / C, f), "c_pmod": np.stack([q % 8, q % 32, q < HD, q >= HD], 1).astype(f), "c_mhalf": np.full((P, 8), -0.5, f),
        "c_cosT": np.ascontiguousarray(np.tile(cos.T, (4, 1))), "c_sinT": np.ascontiguousarray(np.tile(sin.T, (4, 1))),
        "c_cosR": by_row(cos), "c_sinR": by_row(sin),
        "c_idx": np.concatenate([np.arange(NG, 0, -1), np.arange(EPG, 0, -1), BR * np.arange(NE),
                                 np.arange(N_OVER), BR * np.arange(1, MAX_OVER + 1)]).astype(f)[None, :],
        "c_tri": np.where(q[:, None] < q[None, :], 1.0 / C, 0.0).astype(f), "c_zero": np.zeros((1, D), f),
    }


def kernel(**inputs):
    import concourse.bacc as bacc
    from concourse.bass_utils import run_bass_kernel_spmd

    nc = bacc.Bacc("TRN2", target_bir_lowering=False, num_devices=1)
    arrays, args = {}, {}
    for name, x in list((n, np.ascontiguousarray(inputs[n])) for n in WEIGHTS) + list(constants().items()):
        arrays[name] = x
        args[name] = nc.dram_tensor(name, x.shape, mybir.dt.from_np(x.dtype), kind="ExternalInput").ap()
    for name in ("xscratch", "yscratch"):
        args[name] = nc.dram_tensor(name, (NBLK * BR, D), F32).ap()
    args["gscratch"] = nc.dram_tensor("gscratch", (NS_TOK, 3 * NH), F32).ap()
    args["outs"] = {name: nc.dram_tensor("out_" + name, shape, F32, kind="ExternalOutput").ap() for name, shape in OUTS}
    build(nc, args)
    r = run_bass_kernel_spmd(nc, [arrays], core_ids=[0])
    return tuple(r.results[0]["out_" + name] for name, _ in OUTS)
```
